# Optimizing a Trainium2 kernel written in Bass

```python
import math
import jax, jax.numpy as jnp
from jax import lax
import numpy as np

D_MODEL = 1024
BATCH = 1
SEQ = 2048
DEPTH = 1

MEM_LEN = 256
MLA_HEADS = 8
QK_NOPE_DIM = 64
QK_ROPE_DIM = 32
V_HEAD_DIM = 64
Q_LORA_RANK = 256
KV_LORA_RANK = 128
ROPE_THETA = 10000.0
Q_BLOCK = 128
CONV_WIDTH = 512
CONV_KSIZE = 3
XATTN_HEADS = 4
XATTN_HEAD_DIM = 128
N_GROUPS = 8
EXPERTS_PER_GROUP = 8
N_EXPERTS = N_GROUPS * EXPERTS_PER_GROUP
TOP_K_IN_GROUP = 2
EXPERT_FF = 256
DISPATCH_BLOCK = 128
N_BRANCHES = 2
EPS = 1e-6

COL_CQ = Q_LORA_RANK
COL_CKV = COL_CQ + KV_LORA_RANK
COL_KROPE = COL_CKV + QK_ROPE_DIM
COL_CONV = COL_KROPE + 3 * CONV_WIDTH
IN_COLS = COL_CONV + N_BRANCHES * D_MODEL

kernel_name = "hybrid_mla_shortconv_gated_hmoe_block"

def rmsnorm(x, g):
    xf = x.astype(jnp.float32)
    y = xf * lax.rsqrt(jnp.mean(xf * xf, axis=-1, keepdims=True) + EPS)
    return (y * g.astype(jnp.float32)).astype(x.dtype)

def rope_tables(positions):
    inv_freq = ROPE_THETA ** (-jnp.arange(0, QK_ROPE_DIM, 2, dtype=jnp.float32) / QK_ROPE_DIM)
    ang = positions.astype(jnp.float32)[..., None] * inv_freq
    return jnp.cos(ang), jnp.sin(ang)

def apply_rope(x, cos, sin):
    half = x.shape[-1] // 2
    x1 = x[..., :half].astype(jnp.float32)
    x2 = x[..., half:].astype(jnp.float32)
    return jnp.concatenate([x1 * cos - x2 * sin, x1 * sin + x2 * cos], axis=-1).astype(x.dtype)

def mla_attention(c_q, c_kv, k_rope_raw, cos, sin, g_cq, w_uq, g_ckv, w_ukv):
    B, S, _ = c_q.shape
    q = (rmsnorm(c_q, g_cq) @ w_uq).reshape(B, S, MLA_HEADS, QK_NOPE_DIM + QK_ROPE_DIM)
    q_nope = q[..., :QK_NOPE_DIM]
    q_rope = apply_rope(q[..., QK_NOPE_DIM:], cos[:, :, None, :], sin[:, :, None, :])
    kv = (rmsnorm(c_kv, g_ckv) @ w_ukv).reshape(B, S, MLA_HEADS, QK_NOPE_DIM + V_HEAD_DIM)
    k_nope, v = kv[..., :QK_NOPE_DIM], kv[..., QK_NOPE_DIM:]
    k_rope = apply_rope(k_rope_raw, cos, sin)
    scale = 1.0 / math.sqrt(QK_NOPE_DIM + QK_ROPE_DIM)
    outs = []
    for i in range(S // Q_BLOCK):
        q0, q1 = i * Q_BLOCK, (i + 1) * Q_BLOCK
        s = (jnp.einsum("bqhd,bkhd->bhqk", q_nope[:, q0:q1], k_nope[:, :q1])
             + jnp.einsum("bqhr,bkr->bhqk", q_rope[:, q0:q1], k_rope[:, :q1]))
        s = s.astype(jnp.float32) * scale
        causal = jnp.arange(q1)[None, :] <= (q0 + jnp.arange(Q_BLOCK))[:, None]
        p = jax.nn.softmax(jnp.where(causal, s, -jnp.inf), axis=-1).astype(v.dtype)
        outs.append(jnp.einsum("bhqk,bkhd->bqhd", p, v[:, :q1]))
    return jnp.concatenate(outs, axis=1).reshape(B, S, MLA_HEADS * V_HEAD_DIM)

def gated_short_conv(bcx, conv_w):
    b_gate, c_gate, xv = jnp.split(bcx, 3, axis=-1)
    u = c_gate * xv
    S = u.shape[1]
    u_pad = jnp.pad(u, ((0, 0), (CONV_KSIZE - 1, 0), (0, 0)))
    y = conv_w[0] * u_pad[:, 0:S]
    for k in range(1, CONV_KSIZE):
        y = y + conv_w[k] * u_pad[:, k:k + S]
    return b_gate * y

def memory_cross_attention(h, mem_n, w_q, w_kv, w_o):
    B, S, _ = h.shape
    M = mem_n.shape[1]
    q = (h @ w_q).reshape(B, S, XATTN_HEADS, XATTN_HEAD_DIM)
    kv = (mem_n @ w_kv).reshape(B, M, 2, XATTN_HEADS, XATTN_HEAD_DIM)
    k, v = kv[:, :, 0], kv[:, :, 1]
    s = jnp.einsum("bqhd,bmhd->bhqm", q, k).astype(jnp.float32) / math.sqrt(XATTN_HEAD_DIM)
    p = jax.nn.softmax(s, axis=-1).astype(v.dtype)
    o = jnp.einsum("bhqm,bmhd->bqhd", p, v).reshape(B, S, XATTN_HEADS * XATTN_HEAD_DIM)
    return o @ w_o

def hierarchical_moe(h, w_rg, b_rg, w_re, b_re, w_gate_up, w_down):
    B, S, D = h.shape
    N = B * S
    hf = h.reshape(N, D)
    group_logits = (hf @ w_rg).astype(jnp.float32) + b_rg.astype(jnp.float32)
    group_prob = jax.nn.softmax(group_logits, axis=-1)
    _, g_idx = lax.top_k(group_logits, 1)
    p_group = jnp.take_along_axis(group_prob, g_idx, axis=-1)
    exp_logits = ((hf @ w_re).astype(jnp.float32) + b_re.astype(jnp.float32)).reshape(N, N_GROUPS, EXPERTS_PER_GROUP)
    idx = jnp.broadcast_to(g_idx[:, :, None], (N, 1, EXPERTS_PER_GROUP))
    in_group = jnp.take_along_axis(exp_logits, idx, axis=1)[:, 0]
    top_vals, top_local = lax.top_k(in_group, TOP_K_IN_GROUP)
    combine = p_group * jax.nn.softmax(top_vals, axis=-1)
    expert_id = (g_idx * EXPERTS_PER_GROUP + top_local).reshape(-1)
    token_id = jnp.repeat(jnp.arange(N, dtype=jnp.int32), TOP_K_IN_GROUP)
    weight = combine.reshape(-1)
    NK = N * TOP_K_IN_GROUP
    order = jnp.argsort(expert_id)
    e_sorted, tok_sorted, w_sorted = expert_id[order], token_id[order], weight[order]
    counts = jnp.zeros((N_EXPERTS,), jnp.int32).at[expert_id].add(1)
    padded = (counts + DISPATCH_BLOCK - 1) // DISPATCH_BLOCK * DISPATCH_BLOCK
    start = jnp.cumsum(counts) - counts
    pad_end = jnp.cumsum(padded)
    pad_start = pad_end - padded
    dest = pad_start[e_sorted] + (jnp.arange(NK, dtype=jnp.int32) - start[e_sorted])
    P = (NK + DISPATCH_BLOCK - 1) // DISPATCH_BLOCK * DISPATCH_BLOCK + N_EXPERTS * DISPATCH_BLOCK
    n_blocks = P // DISPATCH_BLOCK
    x_disp = jnp.zeros((P, D), h.dtype).at[dest].set(hf[tok_sorted])
    block_expert = jnp.minimum(
        jnp.searchsorted(pad_end, jnp.arange(n_blocks, dtype=jnp.int32) * DISPATCH_BLOCK, side="right"),
        N_EXPERTS - 1)

    def expert_block(args):
        xb, e = args
        gate, up = jnp.split(xb @ w_gate_up[e], 2, axis=-1)
        return (jax.nn.silu(gate) * up) @ w_down[e]

    y_disp = lax.map(expert_block, (x_disp.reshape(n_blocks, DISPATCH_BLOCK, D), block_expert)).reshape(P, D)
    y = jnp.zeros((N, D), h.dtype).at[tok_sorted].add(y_disp[dest] * w_sorted[:, None].astype(h.dtype))
    return y.reshape(B, S, D)

def setup_inputs(seed: int = 0) -> dict:
    key = jax.random.key(seed)
    ks = jax.random.split(key, 32)

    def nrm(k, shape, scale):
        return jax.random.normal(k, shape, jnp.float32) * scale

    def gain(k, n):
        return 1.0 + 0.02 * jax.random.normal(k, (DEPTH, n), jnp.float32)

    offsets = jax.random.randint(ks[2], (BATCH, 1), 0, 4096, dtype=jnp.int32)
    positions = offsets + jnp.arange(SEQ, dtype=jnp.int32)[None, :]
    return {
        "x": nrm(ks[0], (BATCH, SEQ, D_MODEL), 1.0),
        "mem": nrm(ks[1], (BATCH, MEM_LEN, D_MODEL), 1.0),
        "positions": positions,
        "g_mix": gain(ks[3], D_MODEL),
        "w_in": nrm(ks[4], (DEPTH, D_MODEL, IN_COLS), D_MODEL ** -0.5),
        "b_gate": nrm(ks[5], (DEPTH, N_BRANCHES * D_MODEL), 0.02),
        "g_cq": gain(ks[6], Q_LORA_RANK),
        "w_uq": nrm(ks[7], (DEPTH, Q_LORA_RANK, MLA_HEADS * (QK_NOPE_DIM + QK_ROPE_DIM)), Q_LORA_RANK ** -0.5),
        "g_ckv": gain(ks[8], KV_LORA_RANK),
        "w_ukv": nrm(ks[9], (DEPTH, KV_LORA_RANK, MLA_HEADS * (QK_NOPE_DIM + V_HEAD_DIM)), KV_LORA_RANK ** -0.5),
        "conv_w": nrm(ks[10], (DEPTH, CONV_KSIZE, CONV_WIDTH), CONV_KSIZE ** -0.5),
        "w_branch_a": nrm(ks[11], (DEPTH, MLA_HEADS * V_HEAD_DIM, D_MODEL), (MLA_HEADS * V_HEAD_DIM) ** -0.5),
        "w_branch_b": nrm(ks[12], (DEPTH, CONV_WIDTH, D_MODEL), CONV_WIDTH ** -0.5),
        "w_out": nrm(ks[13], (DEPTH, D_MODEL, D_MODEL), D_MODEL ** -0.5),
        "g_xattn": gain(ks[14], D_MODEL),
        "g_mem": gain(ks[15], D_MODEL),
        "w_q_mem": nrm(ks[16], (DEPTH, D_MODEL, XATTN_HEADS * XATTN_HEAD_DIM), D_MODEL ** -0.5),
        "w_kv_mem": nrm(ks[17], (DEPTH, D_MODEL, 2 * XATTN_HEADS * XATTN_HEAD_DIM), D_MODEL ** -0.5),
        "w_o_mem": nrm(ks[18], (DEPTH, XATTN_HEADS * XATTN_HEAD_DIM, D_MODEL), (XATTN_HEADS * XATTN_HEAD_DIM) ** -0.5),
        "g_moe": gain(ks[19], D_MODEL),
        "w_router_group": nrm(ks[20], (DEPTH, D_MODEL, N_GROUPS), D_MODEL ** -0.5),
        "b_router_group": nrm(ks[21], (DEPTH, N_GROUPS), 0.01),
        "w_router_expert": nrm(ks[22], (DEPTH, D_MODEL, N_EXPERTS), D_MODEL ** -0.5),
        "b_router_expert": nrm(ks[23], (DEPTH, N_EXPERTS), 0.01),
        "w_gate_up": nrm(ks[24], (DEPTH, N_EXPERTS, D_MODEL, 2 * EXPERT_FF), D_MODEL ** -0.5),
        "w_down": nrm(ks[25], (DEPTH, N_EXPERTS, EXPERT_FF, D_MODEL), EXPERT_FF ** -0.5),
        "g_final": 1.0 + 0.02 * jax.random.normal(ks[26], (D_MODEL,), jnp.float32),
    }

def reference(x, mem, positions, g_mix, w_in, b_gate, g_cq, w_uq, g_ckv, w_ukv, conv_w,
              w_branch_a, w_branch_b, w_out, g_xattn, g_mem, w_q_mem, w_kv_mem, w_o_mem,
              g_moe, w_router_group, b_router_group, w_router_expert, b_router_expert,
              w_gate_up, w_down, g_final):
    cos, sin = rope_tables(positions)
    for l in range(DEPTH):
        h = rmsnorm(x, g_mix[l])
        proj = h @ w_in[l]
        c_q, c_kv, k_rope_raw, bcx, gate_logits = jnp.split(
            proj, [COL_CQ, COL_CKV, COL_KROPE, COL_CONV], axis=-1)
        attn = mla_attention(c_q, c_kv, k_rope_raw, cos, sin, g_cq[l], w_uq[l], g_ckv[l], w_ukv[l])
        conv = gated_short_conv(bcx, conv_w[l])
        gates = jax.nn.sigmoid((gate_logits + b_gate[l]).astype(jnp.float32)).astype(x.dtype)
        g_a, g_b = jnp.split(gates, N_BRANCHES, axis=-1)
        mixed = g_a * (attn @ w_branch_a[l]) + g_b * (conv @ w_branch_b[l])
        x = x + mixed @ w_out[l]
        x = x + memory_cross_attention(rmsnorm(x, g_xattn[l]), rmsnorm(mem, g_mem[l]),
                                       w_q_mem[l], w_kv_mem[l], w_o_mem[l])
        x = x + hierarchical_moe(rmsnorm(x, g_moe[l]), w_router_group[l], b_router_group[l],
                                 w_router_expert[l], b_router_expert[l], w_gate_up[l], w_down[l])
    return rmsnorm(x, g_final)


_drawn_inputs = setup_inputs


def setup_inputs(seed=0):
    import zlib

    import numpy as np

    out = dict(_drawn_inputs(seed))
    spreads = {}
    factors = {'b_gate': 6.428,
     'g_cq': 8.0,
     'g_ckv': 8.0,
     'g_xattn': 8.0,
     'g_mem': 8.0,
     'g_moe': 2.802,
     'b_router_group': 8.0,
     'b_router_expert': 18.017,
     'g_final': 7.862}
    for name, (base, spread) in spreads.items():
        noise = np.random.default_rng([zlib.crc32(name.encode()), seed]).standard_normal(out[name].shape)
        drawn = base * np.exp(spread * noise) if base else spread * noise
        out[name] = __import__('jax').numpy.asarray(drawn.astype(out[name].dtype))
    for name, factor in factors.items():
        out[name] = (out[name] * factor).astype(out[name].dtype)
    return out
```

```python
import math
from contextlib import ExitStack

import numpy as np
import concourse.bass as bass
from concourse import mybir

P = 128
D = 1024
KD = D // P
T = 2048
NT = T // P
CH = 512
NC_ = T // CH
MEM = 256
H = 8
NOPE, ROPE, VD = 64, 32, 64
QKD = NOPE + ROPE
CW = 512
XH, XD = 4, 128
G, EG = 8, 8
E = G * EG
FF = 256
OVF = T * 2 // P - 1
NB = E + OVF + 1
EPS = 1e-6
NEG = -1e30
TWO_PI_PARTS = (6.28125, 0.00193500518798828125, 3.01991612900e-07)

PI_IN = 3.1415925

ALU = mybir.AluOpType
ACT = mybir.ActivationFunctionType
F32 = mybir.dt.float32
F32R = mybir.dt.float32r
BF16 = mybir.dt.bfloat16
I32 = mybir.dt.int32
U32 = mybir.dt.uint32
AX = mybir.AxisListType.X

C_ID, C_NEG, C_LT, C_IOTA, C_INV, C_SGN, C_E128, C_NEGT, C_ONE, C_END = 0, 128, 256, 384, 448, 449, 450, 514, 642, 645
V_CONV, V_BG, V_CQ, V_CKV, V_END = 0, 12, 28, 30, 31


class Scope:

    def __init__(self, nc, ctx, tag):
        self.nc, self.ctx, self.tag = nc, ctx, tag

    def sb(self, name, shape, dt=F32):
        return self.ctx.enter_context(self.nc.sbuf_tensor(f"{self.tag}_{name}", shape, dt))

    def ps(self, name, shape, dt=F32):
        return self.ctx.enter_context(self.nc.psum_tensor(f"{self.tag}_{name}", shape, dt))

    def sem(self, name):
        return self.ctx.enter_context(self.nc.semaphore(f"{self.tag}_{name}"))

    def kept(self, name):
        return self.nc.alloc_semaphore(f"{self.tag}_{name}")


def clear_semaphores(nc):
    used = sorted(nc.released_uncleared_semaphores)
    with nc.Block() as block:
        @block.gpsimd
        def _(pool):
            runs = []
            for n in used:
                if runs and runs[-1][1] == n:
                    runs[-1][1] = n + 1
                else:
                    runs.append([n, n + 1])
            for a, b in runs:
                pool.sem_clear(range(a, b))


def norm_transpose(nc, tag, cst, src, g, hT, nt, rows_out=None):
    with ExitStack() as ctx:
        s_ = Scope(nc, ctx, tag)
        xr = s_.sb("xr", [P, 2, D])
        xn = s_.sb("xn", [P, 2, D])
        sq = s_.sb("sq", [P, D])
        gb = s_.sb("gb", [P, D])
        st = s_.sb("st", [P, 2, 3])
        eps = s_.sb("eps", [P, 1])
        tp = [s_.ps(f"tp{i}", [P, 4, P]) for i in range(4)]
        x_in = [s_.sem("x_in0"), s_.sem("x_in1")]
        g_in, eps_set, sq_done, rms_done = s_.sem("g_in"), s_.sem("eps_set"), s_.sem("sq_done"), s_.sem("rms_done")
        rcp_done, norm_done, turned = s_.sem("rcp_done"), s_.sem("norm_done"), s_.sem("turned")
        out_a, out_v = s_.sem("out_a"), s_.sem("out_v")
        stored = [s_.sem("stored0"), s_.sem("stored1")]
        ident = cst[:, C_ID:C_ID + P]
        block = ctx.enter_context(nc.Block())

        @block.sync
        def _(sp):
            sp.dma_start(gb[:], g.broadcast_to([P, D])).then_inc(g_in, 16)

            def load(i, s):
                sp.dma_start(xr[:, s, :], src[bass.ts(i, P), :]).then_inc(x_in[s], 16)

            def store(i, n, s):
                sp.wait_ge(norm_done, n)
                if rows_out is not None:
                    sp.dma_start(rows_out[bass.ts(i, P), :], xn[:, s, :]).then_inc(stored[s], 16)

            load(0, 0)
            load(1, 1)
            if nt > 2:
                with sp.Fori(0, nt // 2 - 1) as t:
                    for s in range(2):
                        store(2 * t + s, 2 * t + s + 1, s)
                        load(2 * t + s + 2, s)
            for s in range(2):
                store(nt - 2 + s, nt - 1 + s, s)
            if rows_out is not None:
                for s in range(2):
                    sp.wait_ge(stored[s], 16 * (nt // 2))

        @block.scalar
        def _(act):
            act.wait_ge(eps_set, 1)

            def squares(i, s, t1):
                act.wait_ge(x_in[s], 16 * t1)
                nc.scalar.activation(sq[:], xr[:, s, :], ACT.Square, accum_out=st[:, s, 0:1]).then_inc(sq_done, 1)
                act.wait_ge(sq_done, i + 1)
                nc.scalar.activation(st[:, s, 1:2], st[:, s, 0:1], ACT.Sqrt, bias=eps[:], scale=1.0 / D).then_inc(rms_done, 1)

            def copy_out(i, s):
                act.wait_ge(turned, i + 1)
                nc.scalar.copy(hT[:, 0:4, bass.ts(i, P)], tp[2 * s][:]).then_inc(out_a, 1)

            squares(0, 0, 1)
            if nt > 2:
                with act.Fori(0, nt // 2 - 1) as t:
                    squares(2 * t + 1, 1, t + 1)
                    copy_out(2 * t, 0)
                    squares(2 * t + 2, 0, t + 2)
                    copy_out(2 * t + 1, 1)
            squares(nt - 1, 1, nt // 2)
            copy_out(nt - 2, 0)
            copy_out(nt - 1, 1)

        @block.vector
        def _(dve):
            nc.vector.memset(eps[:], EPS).then_inc(eps_set, 1)
            dve.wait_ge(g_in, 16)

            def norm(i, s, t1, again):
                dve.wait_ge(rms_done, i + 1)
                nc.vector.reciprocal(st[:, s, 2:3], st[:, s, 1:2]).then_inc(rcp_done, 1)
                dve.wait_ge(rcp_done, i + 1)
                if again:
                    dve.wait_ge(turned, i - 1)
                    if rows_out is not None:
                        dve.wait_ge(stored[s], 16 * t1 - 16)
                dve.wait_ge(x_in[s], 16 * t1)
                nc.vector.scalar_tensor_tensor(xn[:, s, :], xr[:, s, :], st[:, s, 2:3], gb[:], ALU.mult, ALU.mult).then_inc(norm_done, 1)

            def copy_out(i, s):
                dve.wait_ge(turned, i + 1)
                nc.vector.tensor_copy(hT[:, 4:8, bass.ts(i, P)], tp[2 * s + 1][:]).then_inc(out_v, 1)

            norm(0, 0, 1, False)
            norm(1, 1, 1, False)
            if nt > 2:
                with dve.Fori(0, nt // 2 - 1) as t:
                    copy_out(2 * t, 0)
                    norm(2 * t + 2, 0, t + 2, True)
                    copy_out(2 * t + 1, 1)
                    norm(2 * t + 3, 1, t + 2, True)
            copy_out(nt - 2, 0)
            copy_out(nt - 1, 1)

        @block.tensor
        def _(pe):
            def turn(i, s, again):
                pe.wait_ge(norm_done, i + 1)
                if again:
                    pe.wait_ge(out_a, i - 1)
                    pe.wait_ge(out_v, i - 1)
                for k in range(KD):
                    mm = nc.tensor.transpose(tp[2 * s + k // 4][:, k % 4, :], xn[:, s, k * P:(k + 1) * P], ident)
                mm.then_inc(turned, 1)

            turn(0, 0, False)
            turn(1, 1, False)
            if nt > 2:
                with pe.Fori(1, nt // 2) as t:
                    for s in range(2):
                        turn(2 * t + s, s, True)


def project(nc, cst, vec, hT, w_in, w_kr, pos, gates_d, conv_d, cqT, ckvT, krT, cosT, sinT):
    with ExitStack() as ctx:
        s_ = Scope(nc, ctx, "pj")
        slab = s_.sb("slab", [P, 2, KD, P])
        gst = s_.sb("gst", [P, 2, T])
        bcx = s_.sb("bcx", [P, 3, T])
        u = s_.sb("u", [P, T + 2])
        y = s_.sb("y", [P, T])
        bias = s_.sb("bias", [P, 2])
        bias_set = s_.sem("bias_set")
        acc = [s_.ps(f"acc{i}", [P, CH]) for i in range(8)]
        w_ready = [s_.sem("w0"), s_.sem("w1")]
        mm_done, evac, y_done, y_out = s_.sem("mm"), s_.sem("evac"), s_.sem("y_done"), s_.kept("y_out")
        angle_step, conv_step, pos_in = s_.sem("angle_step"), s_.sem("conv_step"), s_.sem("pos_in")
        g_out = [s_.kept("g_out0"), s_.kept("g_out1")]
        LAT, CONV, GATE = 4, 3 * CW // P, 2 * D // P
        col0 = w_in.shape[1] - 2 * D - 3 * CW
        posi = gst[:, 0, :].bitcast(I32)
        block = ctx.enter_context(nc.Block())

        @block.sync
        def _(sp):
            def load(src, s, n=P):
                sp.dma_start(slab[:, s, :, 0:n], src.rearrange("(k p) n -> p k n", p=P)).then_inc(w_ready[s], 16)

            sp.dma_start(posi, pos.broadcast_to([P, T])).then_inc(pos_in, 16)
            load(w_in[:, 0:P], 0)
            load(w_in[:, P:2 * P], 1)
            sp.wait_ge(mm_done, 4)
            load(w_in[:, 2 * P:3 * P], 0)
            sp.wait_ge(mm_done, 8)
            load(w_kr, 1, 2 * ROPE)
            with sp.Fori(0, CW // P // 2) as t:
                for q in range(6):
                    sp.wait_ge(mm_done, 4 * (6 * t + q + LAT - 1))
                    load(w_in[:, bass.ds(2 * P * t + (col0 + q % 3 * CW + q // 3 * P), P)], q % 2)
            with sp.Fori(0, GATE // 2) as t:
                for s in range(2):
                    sp.wait_ge(mm_done, 4 * (2 * t + s + LAT + CONV - 1))
                    load(w_in[:, bass.ds(2 * P * t + (col0 + 3 * CW + s * P), P)], s)

        @block.gpsimd
        def _(pool):
            with pool.Fori(0, CW // P) as j:
                pool.wait_ge(y_done, j + 1)
                pool.dma_start(conv_d[bass.ts(j, P), :], y[:]).then_inc(y_out, 16)
            with pool.Fori(0, GATE // 2) as t:
                for s in range(2):
                    pool.wait_ge(evac, 4 * (2 * t + s + LAT + CONV + 1))
                    pool.dma_start(gates_d[bass.ts(2 * t + s, P), :], gst[:, s, :]).then_inc(g_out[s], 16)
            pool.wait_ge(y_out, 16 * (CW // P))
            for s in range(2):
                pool.wait_ge(g_out[s], 16 * (GATE // 2))

        @block.tensor
        def _(pe):
            def run(n, s, again, m=P):
                for c in range(4):
                    if again:
                        pe.wait_ge(evac, 4 * (n - 2) + c + 1)
                    for k in range(KD):
                        mm = nc.tensor.matmul(acc[4 * s + c][0:m, :], slab[:, s, k, 0:m], hT[:, k, c * CH:(c + 1) * CH],
                                              start=(k == 0), stop=(k == KD - 1))
                    mm.then_inc(mm_done, 1)

            for n in range(LAT):
                pe.wait_ge(w_ready[n % 2], 16 * (n // 2 + 1))
                run(n, n % 2, n >= 2, 2 * ROPE if n == 3 else P)
            with pe.Fori(LAT // 2, (LAT + CONV + GATE) // 2) as t:
                for s in range(2):
                    pe.wait_ge(w_ready[s], 16 * t + 16)
                    run(2 * t + s, s, True)

        @block.scalar
        def _(act):
            def take(n, s, dst, m=P, bias=None):
                for c in range(4):
                    act.wait_ge(mm_done, 4 * n + c + 1)
                    o, i = dst[:, c * CH:(c + 1) * CH], acc[4 * s + c][0:m, :]
                    if bias is None:
                        nc.scalar.copy(o, i).then_inc(evac, 1)
                    else:
                        nc.scalar.activation(o, i, ACT.Sigmoid, bias=bias).then_inc(evac, 1)

            take(0, 0, cqT[:, 0, :])
            take(1, 1, cqT[:, 1, :])
            take(2, 0, ckvT[:])
            take(3, 1, krT[0:2 * ROPE, :], 2 * ROPE)
            with act.Fori(0, CW // P // 2) as t:
                for q in range(6):
                    if q % 3 == 0:
                        act.wait_ge(y_done, 2 * t + q // 3)
                    take(6 * t + q + LAT, q % 2, bcx[:, q % 3, :])
            act.wait_ge(angle_step, 1)
            with act.Fori(0, GATE // 2) as t:
                for s in range(2):
                    nc.scalar.copy(bias[:, s:s + 1], vec[:, bass.ds(2 * t + (s + V_BG), 1)]).then_inc(bias_set, 1)
                    act.wait_ge(bias_set, 2 * t + (s + 1))
                    act.wait_ge(g_out[s], 16 * t)
                    take(2 * t + s + LAT + CONV, s, gst[:, s, :], P, bias[:, s:s + 1])

        @block.vector
        def _(dve):
            V = nc.vector
            done = [0]

            def link(ins):
                done[0] += 1
                ins.then_inc(angle_step, 1)
                dve.wait_ge(angle_step, done[0])

            dve.wait_ge(pos_in, 16)
            link(V.tensor_copy(y[:], posi))
            link(V.tensor_scalar(sinT[:], y[:], cst[:, C_INV:C_INV + 1], None, ALU.mult))
            link(V.tensor_scalar(y[:], sinT[:], 1.0 / (2 * math.pi), 12582912.0, ALU.mult, ALU.add))
            link(V.tensor_scalar(y[:], y[:], 12582912.0, None, ALU.subtract))
            for part in TWO_PI_PARTS:
                link(V.scalar_tensor_tensor(sinT[:], y[:], -part, sinT[:], ALU.mult, ALU.add))
            link(V.tensor_scalar(cosT[:], sinT[:], math.pi / 2, None, ALU.add))
            link(V.tensor_scalar(y[:], cosT[:], math.pi, -2 * math.pi, ALU.is_gt, ALU.mult))
            link(V.tensor_tensor(cosT[:], cosT[:], y[:], ALU.add))
            for tab in (cosT, sinT):
                link(V.tensor_scalar(tab[:], tab[:], PI_IN, -PI_IN, ALU.min, ALU.max))
            link(V.memset(u[:, 0:2], 0.0))
            with dve.Fori(0, CW // P) as j:
                dve.wait_ge(evac, 12 * j + 4 * LAT + 12)
                b, c, x = (bcx[:, q, :] for q in range(3))
                wc = [vec[:, bass.ds(3 * j + q, 1)] for q in range(3)]
                V.tensor_tensor(u[:, 2:T + 2], c, x, ALU.mult).then_inc(conv_step, 1)
                dve.wait_ge(conv_step, 4 * j + 1)
                dve.wait_ge(y_out, 16 * j)
                V.tensor_scalar(y[:], u[:, 0:T], wc[0], None, ALU.mult).then_inc(conv_step, 1)
                dve.wait_ge(conv_step, 4 * j + 2)
                for q in (1, 2):
                    V.scalar_tensor_tensor(y[:], u[:, q:T + q], wc[q], y[:], ALU.mult, ALU.add).then_inc(conv_step, 1)
                    dve.wait_ge(conv_step, 4 * j + 2 + q)
                V.tensor_tensor(y[:], y[:], b, ALU.mult).then_inc(y_done, 1)


def latents(nc, cst, vec, cqT, ckvT, krT, cosT, sinT, w_uq, w_uk, w_uv, qn_d, qr_d, kn_d, kr_d, v_d):
    QS = 1.0 / math.sqrt(QKD)
    with ExitStack() as ctx:
        s_ = Scope(nc, ctx, "lt")
        wq = s_.sb("wq", [P, 2, 8 * P])
        wk = s_.sb("wk", [P, 4 * P])
        wv = s_.sb("wv", [P, 4 * P])
        ones = s_.sb("ones", [P, P])
        eps = s_.sb("eps", [P, 1])
        sq = s_.sb("sq", [P, 3, CH])
        rs = s_.sb("rs", [P, 2, CH])
        cn = s_.sb("cn", [P, 3, CH])
        qn = s_.sb("qn", [P, 4, CH])
        kn = s_.sb("kn", [P, 4, CH])
        vv = s_.sb("vv", [P, 4, CH])
        ra = s_.sb("ra", [P, 2, CH])
        rb = s_.sb("rb", [P, 2, CH])
        ka = s_.sb("ka", [ROPE, CH])
        kb = s_.sb("kb", [ROPE, CH])
        psS = [s_.ps(f"psS{i}", [P, CH]) for i in range(2)]
        psR = [s_.ps(f"psR{i}", [P, CH]) for i in range(4)]
        psU = [s_.ps(f"psU{i}", [P, CH]) for i in range(2)]
        w_in, set_, tab, squared, stat, rooted = (s_.sem(n) for n in ("w_in", "set", "tab", "squared", "stat", "rooted"))
        rcp, normed, rope_mm, unit_mm, taken = (s_.sem(n) for n in ("rcp", "normed", "rope_mm", "unit_mm", "taken"))
        rot, rot_done, stored = s_.sem("rot"), s_.sem("rot_done"), s_.sem("stored")
        block = ctx.enter_context(nc.Block())
        NST = 5

        @block.sync
        def _(sp):
            sp.dma_start(wq[:], w_uq.rearrange("(k p) n -> p k n", p=P)).then_inc(w_in, 16)
            sp.dma_start(wk[:], w_uk).then_inc(w_in, 16)
            sp.dma_start(wv[:], w_uv).then_inc(w_in, 16)
            with sp.Fori(0, NC_) as c:
                t = bass.ts(c, CH)
                sp.wait_ge(rot_done, c + 1)
                sp.dma_start(qr_d[:, t].rearrange("(j p) n -> p j n", p=P), ra[:]).then_inc(stored, 16)
                sp.dma_start(kr_d[:, t], ka[:]).then_inc(stored, 16)
                sp.wait_ge(taken, 12 * c + 4)
                sp.dma_start(qn_d[:, t].rearrange("(j p) n -> p j n", p=P), qn[:]).then_inc(stored, 16)
                sp.wait_ge(taken, 12 * c + 8)
                sp.dma_start(kn_d[:, t].rearrange("(j p) n -> p j n", p=P), kn[:]).then_inc(stored, 16)
                sp.wait_ge(taken, 12 * c + 12)
                sp.dma_start(v_d[t, :].rearrange("(j p) n -> p j n", p=P), vv[:]).then_inc(stored, 16)
            sp.wait_ge(stored, 16 * NST * NC_)

        @block.scalar
        def _(act):
            for i, x in enumerate((sinT, cosT)):
                nc.scalar.activation(x[:], x[:], ACT.Sin).then_inc(tab, 1)
            act.wait_ge(set_, 2)
            with act.Fori(0, NC_) as c:
                t = bass.ts(c, CH)
                nc.scalar.activation(sq[:, 0:2, :], cqT[:, :, t], ACT.Square).then_inc(squared, 1)
                nc.scalar.activation(sq[:, 2, :], ckvT[:, t], ACT.Square).then_inc(squared, 1)
                for i, n in enumerate((2 * P, P)):
                    act.wait_ge(stat, 2 * c + i + 1)
                    nc.scalar.activation(rs[:, i, :], psS[i][:], ACT.Sqrt, bias=eps[:], scale=1.0 / n).then_inc(rooted, 1)
                act.wait_ge(stored, 16 * NST * c)
                for u in range(12):
                    act.wait_ge(unit_mm, 12 * c + u + 1)
                    dst = (qn, kn, vv)[u // 4][:, u % 4, :]
                    nc.scalar.activation(dst, psU[u % 2][:], ACT.Copy, scale=QS if u < 4 else 1.0).then_inc(taken, 1)

        @block.vector
        def _(dve):
            V = nc.vector
            V.memset(ones[:], 1.0).then_inc(set_, 1)
            V.memset(eps[:], EPS).then_inc(set_, 1)
            dve.wait_ge(tab, 2)
            V.tensor_scalar(sinT[:], sinT[:], cst[:, C_SGN:C_SGN + 1], None, ALU.mult).then_inc(tab, 1)
            dve.wait_ge(tab, 3)
            with dve.Fori(0, NC_) as c:
                t = bass.ts(c, CH)
                for i in range(2):
                    dve.wait_ge(rooted, 2 * c + i + 1)
                    V.reciprocal(rs[:, i, :], rs[:, i, :]).then_inc(rcp, 1)
                dve.wait_ge(rcp, 2 * c + 2)
                for i in range(3):
                    x = cqT[:, i, t] if i < 2 else ckvT[:, t]
                    V.scalar_tensor_tensor(cn[:, i, :], x, vec[:, V_CQ + i:V_CQ + i + 1], rs[:, i // 2, :],
                                           ALU.mult, ALU.mult).then_inc(normed, 1)
                dve.wait_ge(stored, 16 * NST * c)
                V.tensor_tensor(ka[:], krT[0:ROPE, t], cosT[0:ROPE, t], ALU.mult).then_inc(rot, 1)
                V.tensor_tensor(kb[:], krT[ROPE:2 * ROPE, t], sinT[ROPE:2 * ROPE, t], ALU.mult).then_inc(rot, 1)
                for i in range(4):
                    dve.wait_ge(rope_mm, 4 * c + i + 1)
                    dst, tabl = ((ra, cosT), (rb, sinT))[i % 2]
                    V.scalar_tensor_tensor(dst[:, i // 2, :], psR[i][:], QS, tabl[:, t], ALU.mult, ALU.mult).then_inc(rot, 1)
                dve.wait_ge(rot, 7 * c + 6)
                V.tensor_tensor(ka[:], ka[:], kb[:], ALU.add).then_inc(rot, 1)
                dve.wait_ge(rot, 7 * c + 7)
                V.tensor_tensor(ra[:], ra[:], rb[:], ALU.add).then_inc(rot_done, 1)

        @block.tensor
        def _(pe):
            pe.wait_ge(w_in, 48)
            pe.wait_ge(set_, 2)
            with pe.Fori(0, NC_) as c:
                pe.wait_ge(squared, 2 * c + 1)
                nc.tensor.matmul(psS[0][:], ones[:], sq[:, 0, :], start=True, stop=False)
                nc.tensor.matmul(psS[0][:], ones[:], sq[:, 1, :], start=False, stop=True).then_inc(stat, 1)
                pe.wait_ge(squared, 2 * c + 2)
                nc.tensor.matmul(psS[1][:], ones[:], sq[:, 2, :], start=True, stop=True).then_inc(stat, 1)
                pe.wait_ge(normed, 3 * c + 3)
                pe.wait_ge(rot_done, c)
                for i in range(4):
                    f = (4 + i // 2 + 2 * (i % 2)) * P
                    for k in range(2):
                        mm = nc.tensor.matmul(psR[i][:], wq[:, k, f:f + P], cn[:, k, :], start=(k == 0), stop=(k == 1))
                    mm.then_inc(rope_mm, 1)
                for u in range(12):
                    if u >= 2:
                        pe.wait_ge(taken, 12 * c + u - 1)
                    else:
                        pe.wait_ge(taken, 12 * c)
                    if u < 4:
                        for k in range(2):
                            mm = nc.tensor.matmul(psU[u % 2][:], wq[:, k, u * P:(u + 1) * P], cn[:, k, :], start=(k == 0), stop=(k == 1))
                    elif u < 8:
                        mm = nc.tensor.matmul(psU[u % 2][:], wk[:, (u - 4) * P:(u - 3) * P], cn[:, 2, :], start=True, stop=True)
                    else:
                        mm = nc.tensor.matmul(psU[u % 2][:], cn[:, 2, (u - 8) * P:(u - 7) * P], wv[:], start=True, stop=True)
                    mm.then_inc(unit_mm, 1)


def attention(nc, cst, qn_d, qr_d, kn_d, kr_d, v_d, o_d, l_d):
    rows = [(i, c) for i in range(NT) for c in range(i // 4 + 1)]
    cols = [(c, j) for c in range(NC_) for j in range(4 * c + 4)]
    NU, NA = len(cols), len(rows) + 1
    RING, AHEAD, PIECES = 4, 3, 2 * NC_ + 1
    A0, A1 = 12, 36
    a_at = {}
    for v in range(NA):
        a_at.setdefault(A0 + v * (A1 - A0) // NA, []).append(v)
    KA, VA = QKD + 2, VD + 2
    with ExitStack() as ctx:
        s_ = Scope(nc, ctx, "at")
        qraw = s_.sb("qraw", [QKD, T])
        kraw = s_.sb("kraw", [QKD, T])
        vraw = s_.sb("vraw", [P, NT, VD])
        qh = s_.sb("qh", [KA, 2, T], F32R)
        ql = s_.sb("ql", [QKD, 2, T], F32R)
        kh = s_.sb("kh", [KA, 2, T], F32R)
        kl = s_.sb("kl", [QKD, 2, T], F32R)
        vh = s_.sb("vh", [P, 2, NT, VA], F32R)
        vl = s_.sb("vl", [P, 2, NT, VA], F32R)
        pf = s_.sb("pf", [P, RING, CH])
        ph = s_.sb("ph", [P, RING, CH], F32R)
        pl = s_.sb("pl", [P, RING, CH], F32R)
        ost = s_.sb("ost", [VA, 2, CH])
        nm = s_.sb("nm", [P, NT, 4])
        mm_ = s_.sb("mm", [P, NT])
        mh = s_.sb("mh", [NT, P], F32R)
        ml = s_.sb("ml", [NT, P], F32R)
        idb = s_.sb("idb", [P, P], BF16)
        neg = s_.sb("neg", [P, P], BF16)
        negT = s_.sb("negT", [P, P], BF16)
        psS = [s_.ps(f"psS{i}", [P, CH]) for i in range(RING)]
        psA = [s_.ps(f"psA{i}", [P, CH]) for i in range(2)]
        psO = [s_.ps(f"psO{i}", [P, CH]) for i in range(2)]
        names = ("raw_in", "set", "split_a", "split_p", "st", "ex", "hi", "lo", "pv", "o_out", "a_mm", "a_max", "mmin", "mhd", "mld", "m_in")
        raw_in, set_, split_a, split_p, st, ex, hi, lo, pv, o_out, a_mm, a_max, mmin, mhd, mld, m_in = (s_.sem(n) for n in names)
        o_st = [s_.sem("o_st0"), s_.sem("o_st1")]
        ident = cst[:, C_ID:C_ID + P]
        block = ctx.enter_context(nc.Block())

        def heads(eng, run):
            with eng.Fori(0, H // 2 - 1) as t:
                for s in range(2):
                    run(2 * t + s, s, True)
            run(H - 2, 0, True)
            run(H - 1, 1, False)

        @block.sync
        def _(sp):
            def load(h):
                sp.dma_start(qraw[0:NOPE, :], qn_d[bass.ts(h, NOPE), :]).then_inc(raw_in, 16)
                sp.dma_start(qraw[NOPE:QKD, :], qr_d[bass.ts(h, ROPE), :]).then_inc(raw_in, 16)
                sp.dma_start(kraw[0:NOPE, :], kn_d[bass.ts(h, NOPE), :]).then_inc(raw_in, 16)
                sp.dma_start(kraw[NOPE:QKD, :], kr_d).then_inc(raw_in, 16)
                sp.dma_start(vraw[:], v_d[:, bass.ts(h, VD)].rearrange("(i p) d -> p i d", p=P)).then_inc(raw_in, 16)

            def maxima(h, s):
                sp.wait_ge(mld, h + 1)
                sp.dma_start(qh[QKD:QKD + 1, s, :].bitcast(F32).rearrange("a (i p) -> a i p", p=P), mh[:].bitcast(F32)).then_inc(m_in, 16)
                sp.dma_start(qh[QKD + 1:QKD + 2, s, :].bitcast(F32).rearrange("a (i p) -> a i p", p=P), ml[:].bitcast(F32)).then_inc(m_in, 16)

            def store(h, c):
                sp.wait_ge(o_out, 4 * h + c + 3)
                t = slice(c * CH, (c + 1) * CH)
                sp.dma_start(o_d[bass.ts(h, VD), t], ost[0:VD, c % 2, :]).then_inc(o_st[c % 2], 16)
                sp.dma_start(l_d[bass.ds(h, 1), t], ost[VD:VD + 1, c % 2, :]).then_inc(o_st[c % 2], 16)

            for b in range(2):
                sp.sem_inc(o_st[b], 32)
            sp.sem_inc(m_in, 16)
            load(0)

            def after_split(h):
                sp.wait_ge(split_a, PIECES * h + PIECES)
                sp.wait_ge(split_p, PIECES * h + PIECES)

            after_split(0)
            load(1)
            maxima(0, 0)

            def head(h, s, more, more2):
                if more:
                    store(h, 0)
                    store(h, 1)
                    if more2:
                        after_split(h + 1)
                        load(h + 2)
                    store(h, 2)
                    maxima(h + 1, 1 - s)
                    store(h, 3)
                else:
                    for c in range(NC_):
                        store(h, c)

            with sp.Fori(0, H // 2 - 1) as t:
                for s in range(2):
                    head(2 * t + s, s, True, True)
            head(H - 2, 0, True, False)
            head(H - 1, 1, False, False)
            for b in range(2):
                sp.wait_ge(o_st[b], 32 * (2 * H + 1))

        @block.tensor
        def _(pe):
            def scores(h, s, u, wait_max):
                c, j = cols[u]
                off = max(0, j - 4 * c) * P
                q = slice(c * CH + off, (c + 1) * CH)
                k = slice(j * P, (j + 1) * P)
                out = psS[u % RING][:, off:CH]
                if wait_max:
                    pe.wait_ge(m_in, 32 * h + 48)
                pe.wait_ge(ex, NU * h + u + 1)
                nc.tensor.matmul(out, kh[:, s, k], qh[:, s, q], start=True, stop=False)
                nc.tensor.matmul(out, kh[0:QKD, s, k], ql[:, s, q], start=False, stop=False)
                diag = j >= 4 * c
                mm = nc.tensor.matmul(out, kl[:, s, k], qh[0:QKD, s, q], start=False, stop=not diag)
                if diag:
                    mm = nc.tensor.matmul(psS[u % RING][:, off:off + P], idb[:], negT[:], start=False, stop=True)
                mm.then_inc(st, 1)

            def products(h, s, u):
                c, j = cols[u]
                off = max(0, j - 4 * c) * P
                pe.wait_ge(lo, NU * h + u + 1 + RING)
                if j == 0:
                    pe.wait_ge(o_out, 4 * h + c + 1)
                out = psO[c % 2][0:VA, off:CH]
                last = j == 4 * c + 3
                r = u % RING
                nc.tensor.matmul(out, vh[:, s, j, :], ph[:, r, off:CH], start=(j == 0), stop=False)
                nc.tensor.matmul(out, vh[:, s, j, :], pl[:, r, off:CH], start=False, stop=False)
                nc.tensor.matmul(out, vl[:, s, j, :], ph[:, r, off:CH], start=False, stop=last).then_inc(pv, 1)

            def maxima(h, s, v):
                b = (s * NA + v) % 2
                pe.wait_ge(a_max, NA * h + v + 1)
                if v == NA - 1:
                    pe.wait_ge(mmin, h + 1)
                    nc.tensor.transpose(psA[b][0:NT, 0:P], mm_[:], ident).then_inc(a_mm, 1)
                    return
                i, c = rows[v]
                if v == 0:
                    pe.wait_ge(split_a, PIECES * h + PIECES)
                    pe.wait_ge(split_p, PIECES * h + PIECES)
                w = min(CH, (i + 1) * P - c * CH)
                diag = c == i // 4
                mm = nc.tensor.matmul(psA[b][:, 0:w], qh[0:QKD, s, i * P:(i + 1) * P], kh[0:QKD, s, c * CH:c * CH + w], start=True, stop=not diag)
                if diag:
                    mm = nc.tensor.matmul(psA[b][:, w - P:w], idb[:], neg[:], start=False, stop=True)
                mm.then_inc(a_mm, 1)

            pe.sem_inc(pv, RING)
            pe.wait_ge(set_, 9)
            for v in range(NA):
                maxima(0, 0, v)
            for u in range(AHEAD):
                scores(0, 0, u, u == 0)

            def head(h, s, more):
                for u in range(NU):
                    if u + AHEAD < NU:
                        scores(h, s, u + AHEAD, False)
                    elif more:
                        scores(h + 1, 1 - s, u + AHEAD - NU, u + AHEAD == NU)
                    if more:
                        for v in a_at.get(u, []):
                            maxima(h + 1, 1 - s, v)
                    products(h, s, u)

            heads(pe, head)

        @block.scalar
        def _(act):
            def split(h, s, n):
                if n == 0:
                    act.wait_ge(raw_in, 80 * h + 80)
                if n == PIECES - 1:
                    nc.scalar.copy(vh[:, s, :, 0:VD], vraw[:]).then_inc(split_a, 1)
                    return
                t = slice(n % NC_ * CH, (n % NC_ + 1) * CH)
                d, r = ((qh, qraw), (kh, kraw))[n // NC_]
                nc.scalar.copy(d[0:QKD, s, t], r[:, t]).then_inc(split_a, 1)

            act.sem_inc(ex, RING)
            act.sem_inc(o_out, 2)
            for n in range(PIECES):
                split(0, 0, n)

            def copy_out(h, c):
                act.wait_ge(pv, NU * h + [4, 12, 24, 40][c] + RING)
                act.wait_ge(o_st[c % 2], 64 * h + 32 * (c // 2) + 32)
                nc.scalar.copy(ost[:, c % 2, :], psO[c % 2][0:VA, :]).then_inc(o_out, 1)

            def head(h, s, more):
                for u in range(NU):
                    c, j = cols[u]
                    off = max(0, j - 4 * c) * P
                    act.wait_ge(st, NU * h + u + 1)
                    act.wait_ge(lo, NU * h + u + 1)
                    nc.scalar.activation(pf[:, u % RING, off:CH], psS[u % RING][:, off:CH], ACT.Exp).then_inc(ex, 1)
                    if u in (6, 14, 26):
                        copy_out(h, (6, 14, 26).index(u))
                    if more and u < PIECES:
                        if u == 0:
                            act.wait_ge(pv, NU * h + RING)
                        split(h + 1, 1 - s, u)
                copy_out(h, 3)

            heads(act, head)

        @block.vector
        def _(dve):
            V = nc.vector
            V.tensor_copy(idb[:], cst[:, C_ID:C_ID + P]).then_inc(set_, 1)
            V.tensor_copy(neg[:], cst[:, C_NEG:C_NEG + P]).then_inc(set_, 1)
            V.tensor_copy(negT[:], cst[:, C_NEGT:C_NEGT + P]).then_inc(set_, 1)
            V.tensor_scalar(kh[QKD:KA, :, :], cst[QKD:KA, C_ONE:C_ONE + 1].unsqueeze(2).broadcast_to([2, 2, T]), 1.0, None, ALU.mult).then_inc(set_, 1)
            V.memset(nm[:], -NEG).then_inc(set_, 1)
            dve.sem_inc(lo, RING)
            dve.sem_inc(a_max, 2)

            def top(h, s, v):
                b = (s * NA + v) % 2
                if v < NA - 1:
                    i, c = rows[v]
                    w = min(CH, (i + 1) * P - c * CH)
                    dve.wait_ge(a_mm, NA * h + v + 1)
                    V.tensor_reduce(nm[:, i, c:c + 1], psA[b][:, 0:w], AX, ALU.max, negate=True).then_inc(a_max, 1)
                    return
                dve.wait_ge(a_max, NA * h + v + 2)
                V.tensor_reduce(mm_[:].unsqueeze(2), nm[:], AX, ALU.min).then_inc(mmin, 1)
                dve.wait_ge(a_mm, NA * h + v + 1)
                dve.wait_ge(m_in, 32 * h + 16)
                V.tensor_copy(mh[:], psA[b][0:NT, 0:P]).then_inc(mhd, 1)
                dve.wait_ge(mhd, h + 1)
                V.tensor_tensor(ml[:], psA[b][0:NT, 0:P], mh[:], ALU.subtract).then_inc(a_max, 1)
                dve.wait_ge(a_max, NA * h + v + 3)
                dve.sem_inc(mld, 1)

            for v in range(NA):
                top(0, 0, v)

            def head(h, s, more):
                for u in range(NU):
                    c, j = cols[u]
                    off = max(0, j - 4 * c) * P
                    r = u % RING
                    dve.wait_ge(ex, NU * h + u + 1 + RING)
                    dve.wait_ge(pv, NU * h + u + 1)
                    V.tensor_copy(ph[:, r, off:CH], pf[:, r, off:CH]).then_inc(hi, 1)
                    if more:
                        for v in a_at.get(u, []):
                            top(h + 1, 1 - s, v)

            heads(dve, head)

        @block.gpsimd
        def _(pool):
            G_ = nc.gpsimd
            for s in range(2):
                G_.tensor_copy(vh[:, s, :, VD:VD + 2], cst[:, C_ONE:C_ONE + 2].unsqueeze(1).broadcast_to([P, NT, 2])).then_inc(set_, 1)
                G_.tensor_copy(vl[:, s, :, VD:VD + 2], cst[:, C_ONE + 1:C_ONE + 3].unsqueeze(1).broadcast_to([P, NT, 2])).then_inc(set_, 1)

            def split(h, s, n):
                pool.wait_ge(split_a, PIECES * h + n + 1)
                if n < PIECES - 1:
                    t = slice(n % NC_ * CH, (n % NC_ + 1) * CH)
                    d, x, r = ((ql, qh, qraw), (kl, kh, kraw))[n // NC_]
                    G_.tensor_tensor(d[:, s, t], r[:, t], x[0:QKD, s, t], ALU.subtract).then_inc(split_p, 1)
                else:
                    G_.tensor_tensor(vl[:, s, :, 0:VD], vraw[:], vh[:, s, :, 0:VD], ALU.subtract).then_inc(split_p, 1)

            for n in range(PIECES):
                split(0, 0, n)

            def head(h, s, more):
                for u in range(NU):
                    c, j = cols[u]
                    off = max(0, j - 4 * c) * P
                    r = u % RING
                    pool.wait_ge(hi, NU * h + u + 1)
                    G_.tensor_tensor(pl[:, r, off:CH], pf[:, r, off:CH], ph[:, r, off:CH], ALU.subtract).then_inc(lo, 1)
                    if more and 1 <= u < PIECES + 1:
                        split(h + 1, 1 - s, u - 1)

            heads(pool, head)


def mix(nc, cst, o_d, l_d, conv_d, gates_d, x, w_a, w_b, w_out, x2_d):
    with ExitStack() as ctx:
        s_ = Scope(nc, ctx, "mx")
        wa = s_.sb("wa", [P, 4, D])
        wb = s_.sb("wb", [P, 4, D])
        wo = s_.sb("wo", [P, KD, D])
        ar = s_.sb("ar", [P, 4, CH])
        lr = s_.sb("lr", [P, 4, CH])
        cv = s_.sb("cv", [P, 4, CH])
        aT = s_.sb("aT", [P, 4, CH])
        gt = s_.sb("gt", [P, 4, 2, CH])
        mT = s_.sb("mT", [P, KD, CH])
        m2 = s_.sb("m2", [P, 2, 2, CH])
        xr = s_.sb("xr", [P, 4, D])
        xo = s_.sb("xo", [P, 4, D])
        psAB = [s_.ps(f"psAB{i}", [P, CH]) for i in range(4)]
        psO = [s_.ps(f"psO{i}", [P, CH]) for i in range(2)]
        w_in, ar_in, cv_in, x_in, inverted, flat, ab_done = (s_.sem(n) for n in ("w_in", "ar_in", "cv_in", "x_in", "inverted", "flat", "ab_done"))
        g_in = [s_.sem(f"g_in{i}") for i in range(4)]
        gated, mixed, o_mm, o_done, stored = (s_.sem(n) for n in ("gated", "mixed", "o_mm", "o_done", "stored"))
        ident = cst[:, C_ID:C_ID + P]
        g_v = gates_d.rearrange("(a j p) t -> j p a t", a=2, p=P)
        block = ctx.enter_context(nc.Block())

        @block.sync
        def _(sp):
            def rows(c):
                t = bass.ts(c, CH)
                sp.dma_start(ar[:], o_d[:, t].rearrange("(f p) t -> p f t", p=P)).then_inc(ar_in, 16)
                for e in range(2):
                    sp.dma_start(lr[e * VD:(e + 1) * VD, :, :], l_d[e:H:2, t].unsqueeze(0).broadcast_to([VD, H // 2, CH])).then_inc(ar_in, 16)

            def conv(col):
                sp.dma_start(cv[:], conv_d[:, bass.ds(col, CH)].rearrange("(k p) t -> p k t", p=P)).then_inc(cv_in, 16)

            def gates(col, j):
                sp.dma_start(gt[:, j % 4, :, :], g_v[j, :, :, bass.ds(col, CH)]).then_inc(g_in[j % 4], 16)

            def xrows(c):
                sp.dma_start(xr[:], x[bass.ts(c, CH), :].rearrange("(q p) f -> p q f", p=P)).then_inc(x_in, 16)

            rows(0)
            conv(0)
            for d, w in ((wa, w_a), (wb, w_b)):
                sp.dma_start(d[:], w.rearrange("(k p) n -> p k n", p=P)).then_inc(w_in, 16)
            for j in range(4):
                gates(0, j)
            sp.dma_start(wo[:], w_out.rearrange("(k p) n -> p k n", p=P)).then_inc(w_in, 16)
            xrows(0)
            def chunk(c, last):
                here = sp.snap(c * CH) if not last else c * CH
                if not last:
                    nxt = sp.snap(c * CH + CH)
                for j in range(4):
                    sp.wait_ge(gated, 16 * c + 2 * j + 2)
                    gates(here, j + 4)
                if not last:
                    sp.wait_ge(flat, c + 1)
                    rows(c + 1)
                    for j in range(4):
                        sp.wait_ge(gated, 16 * c + 2 * j + 10)
                        gates(nxt, j)
                    conv(nxt)
                sp.wait_ge(o_done, 8 * c + 8)
                sp.dma_start(x2_d[bass.ts(c, CH), :].rearrange("(q p) f -> p q f", p=P), xo[:]).then_inc(stored, 16)
                if not last:
                    xrows(c + 1)

            with sp.Fori(0, NC_ - 1) as c:
                chunk(c, False)
            chunk(NC_ - 1, True)
            sp.wait_ge(stored, 16 * NC_)

        @block.tensor
        def _(pe):
            with pe.Fori(0, NC_) as c:
                pe.wait_ge(w_in, 48)
                pe.wait_ge(cv_in, 16 * c + 16)
                for j in range(KD):
                    for a in range(2):
                        n = 2 * j + a
                        if a == 1 and j == 0:
                            pe.wait_ge(flat, c + 1)
                        pe.wait_ge(gated, 16 * c + max(n - 3, 0))
                        w, r = ((wb, cv), (wa, aT))[a]
                        for k in range(4):
                            mm = nc.tensor.matmul(psAB[n % 4][:], w[:, k, j * P:(j + 1) * P], r[:, k, :], start=(k == 0), stop=(k == 3))
                        mm.then_inc(ab_done, 1)
                pe.wait_ge(mixed, 8 * c + 8)
                for n in range(8):
                    q, hf = n // 2, n % 2
                    pe.wait_ge(o_done, 8 * c + max(n - 1, 0))
                    for k in range(KD):
                        mm = nc.tensor.matmul(psO[n % 2][:], mT[:, k, q * P:(q + 1) * P], wo[:, k, hf * CH:(hf + 1) * CH], start=(k == 0), stop=(k == KD - 1))
                    mm.then_inc(o_mm, 1)

        @block.vector
        def _(dve):
            V = nc.vector
            with dve.Fori(0, NC_) as c:
                dve.wait_ge(ar_in, 48 * c + 48)
                V.reciprocal(lr[:], lr[:]).then_inc(inverted, 1)
                dve.wait_ge(inverted, c + 1)
                V.tensor_tensor(aT[:], ar[:], lr[:], ALU.mult).then_inc(flat, 1)
                for j in range(KD):
                    dve.wait_ge(g_in[j % 4], 32 * c + 16 * (j // 4) + 16)
                    for a in range(2):
                        n = 2 * j + a
                        dve.wait_ge(ab_done, 16 * c + n + 1)
                        V.tensor_tensor(m2[:, j % 2, a, :], psAB[n % 4][:], gt[:, j % 4, 1 - a, :], ALU.mult).then_inc(gated, 1)
                    dve.wait_ge(gated, 16 * c + 2 * j + 2)
                    dve.wait_ge(o_mm, 8 * c)
                    V.tensor_tensor(mT[:, j, :], m2[:, j % 2, 0, :], m2[:, j % 2, 1, :], ALU.add).then_inc(mixed, 1)
                dve.wait_ge(x_in, 16 * c + 16)
                dve.wait_ge(stored, 16 * c)
                for n in range(8):
                    q, hf = n // 2, slice(n % 2 * CH, n % 2 * CH + CH)
                    dve.wait_ge(o_mm, 8 * c + n + 1)
                    V.tensor_tensor(xo[:, q, hf], psO[n % 2][:], xr[:, q, hf], ALU.add).then_inc(o_done, 1)


def mem_keys_values(nc, memT, w_kv, kmT, vm):
    with ExitStack() as ctx:
        s_ = Scope(nc, ctx, "mk")
        w = s_.sb("w", [P, KD, 2 * XH * XD])
        ps = [s_.ps(f"ps{i}", [P, CH]) for i in range(6)]
        w_in, mm_done, taken = s_.sem("w_in"), s_.sem("mm"), s_.sem("taken")
        block = ctx.enter_context(nc.Block())

        @block.sync
        def _(sp):
            sp.dma_start(w[:], w_kv.rearrange("(k p) n -> p k n", p=P)).then_inc(w_in, 16)

        @block.tensor
        def _(pe):
            pe.wait_ge(w_in, 16)
            for h in range(XH):
                for k in range(KD):
                    mm = nc.tensor.matmul(ps[h][:, 0:MEM], w[:, k, h * XD:(h + 1) * XD], memT[:, k, :], start=(k == 0), stop=(k == KD - 1))
                mm.then_inc(mm_done, 1)
            for b in range(MEM // P):
                for k in range(KD):
                    mm = nc.tensor.matmul(ps[4 + b][:], memT[:, k, b * P:(b + 1) * P], w[:, k, XH * XD:], start=(k == 0), stop=(k == KD - 1))
                mm.then_inc(mm_done, 1)

        @block.vector
        def _(dve):
            for n in range(6):
                dve.wait_ge(mm_done, n + 1)
                if n < 4:
                    nc.vector.tensor_copy(kmT[:, n, :], ps[n][:, 0:MEM]).then_inc(taken, 1)
                else:
                    nc.vector.tensor_copy(vm[:, n - 4, :], ps[n][:]).then_inc(taken, 1)


def cross_attention(nc, cst, hT, kmT, vm, w_q, w_o, x2_d, x3_d, y_d):
    XS = 1.0 / math.sqrt(XD)
    with ExitStack() as ctx:
        s_ = Scope(nc, ctx, "xa")
        wq = s_.sb("wq", [P, KD, XH * XD])
        wo = s_.sb("wo", [P, XH, D])
        qT = s_.sb("qT", [P, XH, CH])
        pr = s_.sb("pr", [P, 2, 2, MEM])
        pT = s_.sb("pT", [P, XH, 2, CH])
        oT = s_.sb("oT", [P, XH, CH])
        xr = s_.sb("xr", [P, 4, D])
        xo = s_.sb("xo", [P, 4, D])
        nm = s_.sb("nm", [P, 8, 2])
        zero = s_.sb("zero", [P, D])
        zero_set, zeroed = s_.sem("zero_set"), s_.sem("zeroed")
        ls = s_.sb("ls", [P, 8, 2])
        psQ = [s_.ps(f"psQ{i}", [P, CH]) for i in range(2)]
        psS = [s_.ps(f"psS{i}", [P, 2, MEM]) for i in range(2)]
        psT = [s_.ps(f"psT{i}", [P, 2, 2, P]) for i in range(2)]
        psO = [s_.ps(f"psO{i}", [P, CH]) for i in range(2)]
        w_in, x_in, q_mm, q_out, scored, maxed, exped = (s_.sem(n) for n in ("w_in", "x_in", "q_mm", "q_out", "scored", "maxed", "exped"))
        rcp, normed, turned, flat, o_mm, o_out, y_mm, y_out, stored = (s_.sem(n) for n in ("rcp", "normed", "turned", "flat", "o_mm", "o_out", "y_mm", "y_out", "stored"))
        ident = cst[:, C_ID:C_ID + P]
        block = ctx.enter_context(nc.Block())

        @block.sync
        def _(sp):
            sp.dma_start(wq[:], w_q.rearrange("(k p) n -> p k n", p=P)).then_inc(w_in, 16)
            sp.dma_start(wo[:], w_o.rearrange("(k p) n -> p k n", p=P)).then_inc(w_in, 16)
            sp.wait_ge(zero_set, 1)
            spare = y_d[E * P:, :].rearrange("(p r) d -> r p d", p=P)
            with sp.Fori(0, NB - E) as r:
                sp.dma_start(spare[bass.ds(r, 1)].rearrange("a p d -> p (a d)"), zero[:]).then_inc(zeroed, 16)
            with sp.Fori(0, NC_) as c:
                sp.wait_ge(y_out, 8 * c)
                sp.dma_start(xr[:], x2_d[bass.ts(c, CH), :].rearrange("(q p) f -> p q f", p=P)).then_inc(x_in, 16)
                sp.wait_ge(y_out, 8 * c + 8)
                sp.dma_start(x3_d[bass.ts(c, CH), :].rearrange("(q p) f -> p q f", p=P), xo[:]).then_inc(stored, 16)
            sp.wait_ge(stored, 16 * NC_)
            sp.wait_ge(zeroed, 16 * (NB - E))

        @block.tensor
        def _(pe):
            pe.wait_ge(w_in, 32)
            with pe.Fori(0, NC_) as c:
                t = bass.ts(c, CH)
                for h in range(XH):
                    pe.wait_ge(q_out, 4 * c + max(h - 1, 0))
                    for k in range(KD):
                        mm = nc.tensor.matmul(psQ[h % 2][:], wq[:, k, h * XD:(h + 1) * XD], hT[:, k, t], start=(k == 0), stop=(k == KD - 1))
                    mm.then_inc(q_mm, 1)
                pe.wait_ge(q_out, 4 * c + 4)

                def score(u):
                    pe.wait_ge(exped, 16 * c + max(2 * u - 2, 0))
                    for e in range(2):
                        h = 2 * (u % 2) + e
                        mm = nc.tensor.matmul(psS[u % 2][:, e, :], qT[:, h, u // 2 * P:u // 2 * P + P], kmT[:, h, :], start=True, stop=True)
                    mm.then_inc(scored, 1)

                score(0)
                score(1)
                for u in range(8):
                    pe.wait_ge(normed, 8 * c + u + 1)
                    pe.wait_ge(flat, 8 * c + max(u - 1, 0))
                    for e in range(2):
                        for b in range(2):
                            mm = nc.tensor.transpose(psT[u % 2][:, e, b, :], pr[:, u % 2, e, b * P:(b + 1) * P], ident)
                    mm.then_inc(turned, 1)
                    if u + 2 < 8:
                        score(u + 2)
                pe.wait_ge(flat, 8 * c + 8)
                for h in range(XH):
                    if h >= 2:
                        pe.wait_ge(o_out, 4 * c + h - 1)
                    else:
                        pe.wait_ge(y_out, 8 * c)
                    for b in range(2):
                        mm = nc.tensor.matmul(psO[h % 2][:], vm[:, b, h * XD:(h + 1) * XD], pT[:, h, b, :], start=(b == 0), stop=(b == 1))
                    mm.then_inc(o_mm, 1)
                pe.wait_ge(o_out, 4 * c + 4)
                for n in range(8):
                    q, hf = n // 2, n % 2
                    pe.wait_ge(y_out, 8 * c + max(n - 1, 0))
                    for k in range(XH):
                        mm = nc.tensor.matmul(psO[n % 2][:], oT[:, k, q * P:(q + 1) * P], wo[:, k, hf * CH:(hf + 1) * CH], start=(k == 0), stop=(k == XH - 1))
                    mm.then_inc(y_mm, 1)

        @block.scalar
        def _(act):
            with act.Fori(0, NC_) as c:
                for h in range(XH):
                    act.wait_ge(q_mm, 4 * c + h + 1)
                    nc.scalar.mul(qT[:, h, :], psQ[h % 2][:], XS).then_inc(q_out, 1)
                for u in range(8):
                    act.wait_ge(maxed, 8 * c + u + 1)
                    act.wait_ge(turned, 8 * c + max(u - 1, 0))
                    for e in range(2):
                        nc.scalar.activation(pr[:, u % 2, e, :], psS[u % 2][:, e, :], ACT.Exp, bias=nm[:, u, e:e + 1],
                                             accum_out=ls[:, u, e:e + 1]).then_inc(exped, 1)
                for h in range(XH):
                    act.wait_ge(o_mm, 4 * c + h + 1)
                    nc.scalar.copy(oT[:, h, :], psO[h % 2][:]).then_inc(o_out, 1)

        @block.vector
        def _(dve):
            V = nc.vector
            V.memset(zero[:], 0.0).then_inc(zero_set, 1)
            with dve.Fori(0, NC_) as c:
                def top(u):
                    dve.wait_ge(scored, 8 * c + u + 1)
                    V.tensor_reduce(nm[:, u, :], psS[u % 2][:], AX, ALU.max, negate=True).then_inc(maxed, 1)

                def norm(u):
                    dve.wait_ge(exped, 16 * c + 2 * u + 2)
                    V.reciprocal(ls[:, u, :], ls[:, u, :]).then_inc(rcp, 1)
                    dve.wait_ge(rcp, 8 * c + u + 1)
                    V.tensor_tensor(pr[:, u % 2, :, :], pr[:, u % 2, :, :], ls[:, u, :].unsqueeze(2).broadcast_to([P, 2, MEM]), ALU.mult).then_inc(normed, 1)

                def flatten(u):
                    dve.wait_ge(turned, 8 * c + u + 1)
                    h = 2 * (u % 2)
                    V.tensor_copy(pT[:, h:h + 2, :, u // 2 * P:u // 2 * P + P], psT[u % 2][:]).then_inc(flat, 1)

                top(0)
                for u in range(8):
                    if u + 1 < 8:
                        top(u + 1)
                    norm(u)
                    if u >= 1:
                        flatten(u - 1)
                flatten(7)
                dve.wait_ge(x_in, 16 * c + 16)
                dve.wait_ge(stored, 16 * c)
                for n in range(8):
                    q, hf = n // 2, slice(n % 2 * CH, n % 2 * CH + CH)
                    dve.wait_ge(y_mm, 8 * c + n + 1)
                    V.tensor_tensor(xo[:, q, hf], psO[n % 2][:], xr[:, q, hf], ALU.add).then_inc(y_out, 1)


def route(nc, cst, hT, w_r, b_r, tab_d, wts, dest, tab, meta):
    NR = G + E
    with ExitStack() as ctx:
        s_ = Scope(nc, ctx, "rt")
        wr = s_.sb("wr", [P, KD, NR])
        br = s_.sb("br", [P, NR])
        lT = s_.sb("lT", [NR, T])
        lg = s_.sb("lg", [P, NT, NR])
        gm = s_.sb("gm", [P, NT, 8])
        pg = s_.sb("pg", [P, NT, G])
        eq = s_.sb("eq", [P, NT, 8])
        ci = s_.sb("ci", [P, NT, 1])
        ohg = s_.sb("ohg", [P, NT, 8])
        oh = s_.sb("oh", [P, 2, NT, 8])
        ing = s_.sb("ing", [P, NT, 8])
        big = s_.sb("big", [P, NT, E])
        asg = s_.sb("asg", [P, 2, NT, E])
        mb = s_.sb("mb", [P, NT, E], BF16)
        cp = s_.sb("cp", [P, NT + 1, E], BF16)
        ones = s_.sb("ones", [P, P], BF16)
        ltb = s_.sb("ltb", [P, P], BF16)
        D_ = s_.sb("D_", [P, NT, E])
        cnt = s_.sb("cnt", [P, 8, E])
        cnti = s_.sb("cnti", [P, E], I32)
        df = s_.sb("df", [P, 2, NT])
        d2 = s_.sb("d2", [P, 2, NT], I32)
        df2 = s_.sb("df2", [P, 2, NT])
        tp = s_.sb("tp", [P, 2, NT], I32)
        tok = s_.sb("tok", [P, NT], I32)
        cmp = s_.sb("cmp", [1, 32, E])
        mf = s_.sb("mf", [1, 40])
        zt = s_.sb("zt", [P, 96], I32)
        psL = [s_.ps(f"psL{i}", [P, CH]) for i in range(4)]
        psR = [s_.ps(f"psR{i}", [P, CH]) for i in range(3)]
        psK = s_.ps("psK", [P, CH])
        w_in, mm_l, lt_out, mm_r, step_, ex, mm_k, zero_in, ready, back, zeroed, mset = (s_.sem(n) for n in (
            "w_in", "mm_l", "lt_out", "mm_r", "step", "ex", "mm_k", "zero_in", "ready", "back", "zeroed", "mset"))
        scat = s_.kept("scat")
        group_ready, pair_ready, tok_set = s_.sem("group_ready"), s_.sem("pair_ready"), s_.sem("tok_set")
        block = ctx.enter_context(nc.Block())
        tab_rows = tab_d.rearrange("(p b) o -> p (b o)", p=P)

        @block.sync
        def _(sp):
            sp.dma_start(wr[:], w_r.rearrange("(k p) n -> p k n", p=P)).then_inc(w_in, 16)
            sp.dma_start(br[:], b_r.broadcast_to([P, NR])).then_inc(w_in, 16)
            sp.wait_ge(zeroed, 1)
            sp.dma_start(tab_rows, zt[:]).then_inc(zero_in, 16)
            sp.wait_ge(scat, 16 * 2 * NT)
            sp.dma_start(tab[:], tab_rows).then_inc(back, 16)
            sp.wait_ge(back, 16)

        @block.tensor
        def _(pe):
            pe.wait_ge(w_in, 32)
            for c in range(4):
                for k in range(KD):
                    mm = nc.tensor.matmul(psL[c][0:NR, :], wr[:, k, :], hT[:, k, c * CH:(c + 1) * CH], start=(k == 0), stop=(k == KD - 1))
                mm.then_inc(mm_l, 1)
            for i in range(NT):
                if i % 4 == 0:
                    pe.wait_ge(lt_out, i // 4 + 1)
                mm = nc.tensor.transpose(psR[i // 6][:, i % 6 * NR:i % 6 * NR + NR], lT[:, i * P:(i + 1) * P], cst[0:NR, C_ID:C_ID + NR])
            mm.then_inc(mm_r, 1)
            pe.wait_ge(ready, 1)
            for q in range(2):
                nc.tensor.matmul(psL[q][:], ltb[:], mb[:, 8 * q:8 * q + 8, :], start=True, stop=False)
                nc.tensor.matmul(psL[q][:], ones[:], cp[:, 8 * q:8 * q + 8, :], start=False, stop=True)
            nc.tensor.matmul(psK[:, 0:E], ones[:], cp[:, NT, :], start=True, stop=True).then_inc(mm_k, 1)

        @block.scalar
        def _(act):
            act.wait_ge(group_ready, 1)
            nc.scalar.activation(pg[:], pg[:], ACT.Exp).then_inc(ex, 1)
            act.wait_ge(pair_ready, 1)
            nc.scalar.activation(gm[:, :, 2:3], gm[:, :, 2:3], ACT.Exp).then_inc(ex, 1)

        @block.vector
        def _(dve):
            V = nc.vector
            n = [0]

            def link(ins):
                n[0] += 1
                ins.then_inc(step_, 1)
                dve.wait_ge(step_, n[0])

            def bc(x, shape):
                return x.broadcast_to(shape)

            link(V.memset(zt[:], 0))
            dve.sem_inc(zeroed, 1)
            link(V.memset(ones[:], 1.0))
            link(V.tensor_copy(ltb[:], cst[:, C_LT:C_LT + P]))
            for c in range(4):
                dve.wait_ge(mm_l, c + 1)
                V.tensor_copy(lT[:, c * CH:(c + 1) * CH], psL[c][0:NR, :]).then_inc(lt_out, 1)
            dve.wait_ge(mm_r, 1)
            dve.wait_ge(w_in, 32)
            for r in range(3):
                m = min(6, NT - 6 * r)
                link(V.tensor_tensor(lg[:, 6 * r:6 * r + m, :], psR[r][:, 0:m * NR].rearrange("p (a b) -> p a b", b=NR),
                                     br[:].unsqueeze(1).broadcast_to([P, m, NR]), ALU.add))
            S8 = [P, NT, 8]
            iota8 = cst[:, C_IOTA:C_IOTA + 8].unsqueeze(1).broadcast_to(S8)

            def pick(vals, mx, out):
                link(V.tensor_tensor(eq[:], vals, bc(mx, S8), ALU.is_equal))
                link(V.scalar_tensor_tensor(eq[:], eq[:], -64.0, iota8, ALU.mult, ALU.add))
                link(V.tensor_reduce(ci[:], eq[:], AX, ALU.min))
                link(V.tensor_scalar(ci[:], ci[:], 64.0, None, ALU.add))
                link(V.tensor_tensor(out, iota8, bc(ci[:], S8), ALU.is_equal))

            gl = lg[:, :, 0:G]
            link(V.tensor_reduce(gm[:, :, 0:1], gl, AX, ALU.max))
            link(V.tensor_tensor(pg[:], gl, bc(gm[:, :, 0:1], S8), ALU.subtract))
            dve.sem_inc(group_ready, 1)
            pick(gl, gm[:, :, 0:1], ohg[:])
            el = lg[:, :, G:].rearrange("p t (g e) -> p t g e", g=G)
            b4 = big[:].rearrange("p t (g e) -> p t g e", g=G)
            S4 = [P, NT, G, EG]
            link(V.tensor_tensor(b4, el, ohg[:].unsqueeze(3).broadcast_to(S4), ALU.mult))
            link(V.tensor_reduce(ing[:], big[:].rearrange("p t (g e) -> p t e g", g=G), AX, ALU.add))
            link(V.tensor_reduce(gm[:, :, 1:2], ing[:], AX, ALU.max))
            pick(ing[:], gm[:, :, 1:2], oh[:, 0])
            link(V.scalar_tensor_tensor(ing[:], oh[:, 0], NEG, ing[:], ALU.mult, ALU.add))
            link(V.tensor_reduce(gm[:, :, 2:3], ing[:], AX, ALU.max))
            pick(ing[:], gm[:, :, 2:3], oh[:, 1])
            link(V.tensor_tensor(gm[:, :, 2:3], gm[:, :, 2:3], gm[:, :, 1:2], ALU.subtract))
            dve.sem_inc(pair_ready, 1)
            for a in range(2):
                link(V.tensor_tensor(asg[:, a].rearrange("p t (g e) -> p t g e", g=G), ohg[:].unsqueeze(3).broadcast_to(S4),
                                     oh[:, a].unsqueeze(2).broadcast_to(S4), ALU.mult))
            link(V.tensor_tensor(mb[:], asg[:, 0], asg[:, 1], ALU.add))
            link(V.memset(cp[:, 0, :], 0.0))
            for i in range(NT):
                link(V.tensor_tensor(cp[:, i + 1, :], cp[:, i, :], mb[:, i, :], ALU.add))
            dve.sem_inc(ready, 1)
            dve.wait_ge(ex, 2)
            link(V.tensor_reduce(gm[:, :, 3:4], pg[:], AX, ALU.add))
            link(V.tensor_scalar(gm[:, :, 4:5], gm[:, :, 2:3], 1.0, None, ALU.add))
            link(V.tensor_tensor(gm[:, :, 3:4], gm[:, :, 3:4], gm[:, :, 4:5], ALU.mult))
            link(V.reciprocal(wts[:, :, 0:1], gm[:, :, 3:4]))
            link(V.tensor_tensor(wts[:, :, 1:2], wts[:, :, 0:1], gm[:, :, 2:3], ALU.mult))
            dve.wait_ge(mm_k, 1)
            link(V.tensor_scalar(cnti[:], psK[:, 0:E], 127.0, None, ALU.add))
            link(V.tensor_scalar(cnti[:], cnti[:], 7, None, ALU.arith_shift_right))
            link(V.tensor_copy(cnt[:, 0, :], cnti[:]))
            link(V.tensor_scalar(cnt[:, 0, :], cnt[:, 0, :], 1.0, 0.0, ALU.subtract, ALU.max))
            link(V.tensor_copy(cnt[:, 1, :], cnt[:, 0, :]))
            for d in range(6):
                a, b, w = 1 + d % 2, 2 - d % 2, 1 << d
                link(V.tensor_copy(cnt[:, b, 0:w], cnt[:, a, 0:w]))
                link(V.tensor_tensor(cnt[:, b, w:], cnt[:, a, w:], cnt[:, a, 0:E - w], ALU.add))
            link(V.tensor_tensor(cnt[:, 3, :], cnt[:, 1, :], cnt[:, 0, :], ALU.subtract))
            link(V.tensor_scalar(cnt[:, 3, :], cnt[:, 3, :], float(E - 1), float(P), ALU.add, ALU.mult))
            link(V.tensor_tensor(cnt[:, 3, :], cnt[:, 3, :], cst[:, C_E128:C_E128 + E], ALU.subtract))
            for q in range(2):
                sl = slice(8 * q, 8 * q + 8)
                rk = psL[q][:].rearrange("p (t e) -> p t e", e=E)
                S3 = [P, 8, E]
                link(V.scalar_tensor_tensor(D_[:, sl, :], rk, float(P), cnt[:, 3, :].unsqueeze(1).broadcast_to(S3), ALU.is_ge, ALU.mult))
                link(V.tensor_tensor(D_[:, sl, :], D_[:, sl, :], rk, ALU.add))
            link(V.tensor_tensor(D_[:], D_[:], cst[:, C_E128:C_E128 + E].unsqueeze(1).broadcast_to([P, NT, E]), ALU.add))
            for a in range(2):
                link(V.tensor_tensor(big[:], asg[:, a], D_[:], ALU.mult))
                link(V.tensor_reduce(df[:, a, :].unsqueeze(2), big[:], AX, ALU.add))
            link(V.tensor_copy(dest[:], df[:]))
            link(V.tensor_scalar(d2[:], dest[:], 7, None, ALU.arith_shift_right))
            link(V.tensor_copy(df2[:], d2[:]))
            link(V.scalar_tensor_tensor(df[:], df2[:], -float(P), df[:], ALU.mult, ALU.add))
            link(V.scalar_tensor_tensor(df[:], df[:], 96.0, df2[:], ALU.mult, ALU.add))
            link(V.tensor_copy(tp[:], df[:]))
            io32 = cst[0:1, C_IOTA:C_IOTA + 32].unsqueeze(2).broadcast_to([1, 32, E])
            link(V.tensor_tensor(cmp[:], cnt[0:1, 1, :].unsqueeze(1).broadcast_to([1, 32, E]), io32, ALU.is_le))
            link(V.tensor_reduce(mf[:, 0:32].unsqueeze(2), cmp[:], AX, ALU.add))
            link(V.tensor_scalar(mf[:, 0:32], mf[:, 0:32], float(E - 1), None, ALU.min))
            link(V.tensor_copy(mf[:, 32:33], cnt[0:1, 1, E - 1:E]))
            link(V.tensor_copy(meta[:, 0:33], mf[:, 0:33]))
            dve.sem_inc(mset, 1)

        @block.gpsimd
        def _(pool):
            nc.gpsimd.iota(tok[:], [[P, NT]], base=0, channel_multiplier=1).then_inc(tok_set, 1)
            pool.wait_ge(tok_set, 1)
            pool.wait_ge(mset, 1)
            pool.wait_ge(zero_in, 16)
            for a in range(2):
                for i in range(NT):
                    nc.gpsimd.indirect_dma_start(tab_d, bass.IndirectOffsetOnAxis(ap=tp[:, a, i:i + 1].bitcast(U32), axis=0), tok[:, i:i + 1], None).then_inc(scat, 16)


def experts(nc, cst, h_d, w_gu, w_dn, y_d, tab, meta):
    with ExitStack() as ctx:
        s_ = Scope(nc, ctx, "ex")
        wg = s_.sb("wg", [P, 2, KD, 2 * FF])
        wd = s_.sb("wd", [P, 2, 2, D])
        ix = s_.sb("ix", [P, 2], I32)
        idle = s_.sb("idle", [1, 8])
        idle_set = s_.sem("idle_set")
        xg = s_.sb("xg", [P, 2, D])
        xT = s_.sb("xT", [P, 2, KD, P])
        sg = s_.sb("sg", [P, 2, FF])
        hm = s_.sb("hm", [P, 2, FF])
        hT = s_.sb("hT", [P, 2, 2, P])
        y = s_.sb("y", [P, 2, D])
        psX = [s_.ps(f"psX{i}", [P, 4, P]) for i in range(2)]
        psG = [s_.ps(f"psG{i}", [P, 2 * FF]) for i in range(2)]
        psH = s_.ps("psH", [P, 2, P])
        psY = [s_.ps(f"psY{i}", [P, CH]) for i in range(2)]
        g_in = [s_.sem("g_in0"), s_.sem("g_in1")]
        d_in = [s_.sem("d_in0"), s_.sem("d_in1")]
        x_in = [s_.kept("x_in0"), s_.kept("x_in1")]
        st = [s_.sem("st0"), s_.sem("st1")]
        ixd, turned, xa, xv, up, sig, gt, hid, hturn, hcopy, down, ya, yv = (s_.sem(n) for n in (
            "ixd", "turned", "xa", "xv", "up", "sig", "gt", "hid", "hturn", "hcopy", "down", "ya", "yv"))
        ident = cst[:, C_ID:C_ID + P]
        block = ctx.enter_context(nc.Block())

        def overflow(eng, run):
            n_ovf = eng.value_load(meta[0:1, 32:33], min_val=0, max_val=OVF)
            with eng.Fori(0, OVF) as o:
                with eng.If(o < n_ovf):
                    run(o + E)

        @block.sync
        def _(sp):
            def load(e, s):
                sp.dma_start(wg[:, s], w_gu[e].rearrange("(k p) n -> p k n", p=P)).then_inc(g_in[s], 16)
                sp.dma_start(wd[:, s], w_dn[e].rearrange("(k p) n -> p k n", p=P)).then_inc(d_in[s], 16)

            def dyn(e, s, n_up, n_down):
                sp.wait_ge(up, n_up)
                sp.dma_start(wg[:, s], w_gu[bass.ds(e, 1)].rearrange("a (k p) n -> p (a k) n", p=P)).then_inc(g_in[s], 16)
                sp.wait_ge(down, n_down)
                sp.dma_start(wd[:, s], w_dn[bass.ds(e, 1)].rearrange("a (k p) n -> p (a k) n", p=P)).then_inc(d_in[s], 16)

            load(0, 0)
            load(1, 1)
            with sp.Fori(0, E // 2 - 1) as t:
                for s in range(2):
                    dyn(2 * t + (s + 2), s, 2 * t + (s + 1), 2 * t + (s + 1))

            def more(b):
                e = sp.value_load(meta[0:1, bass.ds(b - E, 1)], min_val=0, max_val=E - 1)
                dyn(e, 0, b, b)

            overflow(sp, more)

        @block.gpsimd
        def _(pool):
            def gather(b, s, first=False):
                if not first:
                    pool.wait_ge(turned, b - 1)
                nc.gpsimd.tensor_copy(ix[:, s:s + 1], tab[:, bass.ds(b, 1)]).then_inc(ixd, 1)
                pool.wait_ge(ixd, b + 1)
                nc.gpsimd.tensor_tensor(idle[:], idle[:], idle[:], ALU.add)
                nc.gpsimd.indirect_dma_start(xg[:, s, :], None, h_d, bass.IndirectOffsetOnAxis(ap=ix[:, s:s + 1].bitcast(U32), axis=0)).then_inc(x_in[s], 16)

            nc.gpsimd.memset(idle[:], 0.0).then_inc(idle_set, 1)
            pool.wait_ge(idle_set, 1)
            gather(0, 0, True)
            gather(1, 1, True)
            with pool.Fori(1, E // 2) as t:
                for s in range(2):
                    gather(2 * t + s, s)

            def more(b):
                pool.wait_ge(turned, b)
                gather(b, 0)

            overflow(pool, more)

        @block.tensor
        def _(pe):
            def turn(b, s, nx, first=False):
                pe.wait_ge(x_in[s], nx)
                if not first:
                    pe.wait_ge(xa, b)
                    pe.wait_ge(xv, b)
                for k in range(KD):
                    mm = nc.tensor.transpose(psX[k // 4][:, k % 4, :], xg[:, s, k * P:(k + 1) * P], ident)
                mm.then_inc(turned, 1)

            def gate_up(b, s, nw, free=None):
                pe.wait_ge(g_in[s], nw)
                pe.wait_ge(xa, b + 1)
                pe.wait_ge(xv, b + 1)
                if free is not None:
                    pe.wait_ge(hid, free)
                for k in range(KD):
                    mm = nc.tensor.matmul(psG[s][:], xT[:, s, k, :], wg[:, s, k, :], start=(k == 0), stop=(k == KD - 1))
                mm.then_inc(up, 1)

            def turn_hidden(b, s):
                pe.wait_ge(hid, b + 1)
                pe.wait_ge(hcopy, b)
                for k in range(2):
                    mm = nc.tensor.transpose(psH[:, k, :], hm[:, s, k * P:(k + 1) * P], ident)
                mm.then_inc(hturn, 1)

            def go_down(b, s, nw):
                pe.wait_ge(d_in[s], nw)
                pe.wait_ge(hcopy, b + 1)
                pe.wait_ge(ya, b)
                pe.wait_ge(yv, b)
                for f in range(2):
                    for k in range(2):
                        mm = nc.tensor.matmul(psY[f][:], hT[:, s, k, :], wd[:, s, k, f * CH:(f + 1) * CH], start=(k == 0), stop=(k == 1))
                mm.then_inc(down, 1)

            turn(0, 0, 16, True)
            gate_up(0, 0, 16)
            turn(1, 1, 16)
            with pe.Fori(0, E // 2 - 1) as t:
                for s in (1, 0):
                    b = 2 * t + (2 - s)
                    prev = 2 * t + (1 - s)
                    gate_up(b, s, 16 * t + 16 * (2 - s), prev)
                    turn_hidden(prev, 1 - s)
                    turn(2 * t + (3 - s), 1 - s, 16 * t + 32)
                    go_down(prev, 1 - s, 16 * t + 16)
            gate_up(E - 1, 1, 16 * (E // 2), E - 2)
            turn_hidden(E - 2, 0)
            go_down(E - 2, 0, 16 * (E // 2))
            turn_hidden(E - 1, 1)
            go_down(E - 1, 1, 16 * (E // 2))

            def more(b):
                nw = 16 * (b - E) + 16 * (E // 2 + 1)
                turn(b, 0, nw)
                gate_up(b, 0, nw, b)
                turn_hidden(b, 0)
                go_down(b, 0, nw)

            overflow(pe, more)

        @block.scalar
        def _(act):
            def take_x(b, s, first=False):
                act.wait_ge(turned, b + 1)
                if not first:
                    act.wait_ge(up, b - 1)
                nc.scalar.copy(xT[:, s, 0:4, :], psX[0][:]).then_inc(xa, 1)

            def sigmoid(b, s):
                act.wait_ge(up, b + 1)
                nc.scalar.activation(sg[:, s, :], psG[s][:, 0:FF], ACT.Sigmoid).then_inc(sig, 1)

            def take_h(b, s):
                act.wait_ge(hturn, b + 1)
                nc.scalar.copy(hT[:, s], psH[:]).then_inc(hcopy, 1)

            def take_y(b, s, n):
                act.wait_ge(down, b + 1)
                act.wait_ge(st[s], n)
                nc.scalar.copy(y[:, s, 0:CH], psY[0][:]).then_inc(ya, 1)
                act.wait_ge(ya, b + 1)
                act.wait_ge(yv, b + 1)
                act.dma_start(y_d[bass.ts(b, P), :], y[:, s, :]).then_inc(st[s], 16)

            take_x(0, 0, True)
            sigmoid(0, 0)
            take_x(1, 1, True)
            with act.Fori(0, E // 2 - 1) as t:
                for s in (1, 0):
                    prev = 2 * t + (1 - s)
                    sigmoid(2 * t + (2 - s), s)
                    take_h(prev, 1 - s)
                    take_x(2 * t + (3 - s), 1 - s)
                    take_y(prev, 1 - s, 16 * t)
            sigmoid(E - 1, 1)
            take_h(E - 2, 0)
            take_y(E - 2, 0, 16 * (E // 2 - 1))
            take_h(E - 1, 1)
            take_y(E - 1, 1, 16 * (E // 2 - 1))
            act.wait_ge(st[0], 16 * (E // 2))
            act.wait_ge(st[1], 16 * (E // 2))

            def more(b):
                take_x(b, 0)
                sigmoid(b, 0)
                take_h(b, 0)
                n = 16 * (b - E) + 16 * (E // 2)
                take_y(b, 0, n)
                act.wait_ge(st[0], n + 16)
                nc.scalar.copy(sg[0:1, 0, 0:8], cst[0:1, 0:8])

            overflow(act, more)

        @block.vector
        def _(dve):
            V = nc.vector

            def take_x(b, s, first=False):
                dve.wait_ge(turned, b + 1)
                if not first:
                    dve.wait_ge(up, b - 1)
                V.tensor_copy(xT[:, s, 4:8, :], psX[1][:]).then_inc(xv, 1)

            def hidden(b, s):
                dve.wait_ge(sig, b + 1)
                V.tensor_tensor(sg[:, s, :], psG[s][:, 0:FF], sg[:, s, :], ALU.mult).then_inc(gt, 1)
                dve.wait_ge(gt, b + 1)
                V.tensor_tensor(hm[:, s, :], psG[s][:, FF:], sg[:, s, :], ALU.mult).then_inc(hid, 1)

            def take_y(b, s, n):
                dve.wait_ge(down, b + 1)
                dve.wait_ge(st[s], n)
                V.tensor_copy(y[:, s, CH:], psY[1][:]).then_inc(yv, 1)

            take_x(0, 0, True)
            hidden(0, 0)
            take_x(1, 1, True)
            with dve.Fori(0, E // 2 - 1) as t:
                for s in (1, 0):
                    prev = 2 * t + (1 - s)
                    hidden(2 * t + (2 - s), s)
                    take_x(2 * t + (3 - s), 1 - s)
                    take_y(prev, 1 - s, 16 * t)
            hidden(E - 1, 1)
            take_y(E - 2, 0, 16 * (E // 2 - 1))
            take_y(E - 1, 1, 16 * (E // 2 - 1))

            def more(b):
                take_x(b, 0)
                hidden(b, 0)
                take_y(b, 0, 16 * (b - E) + 16 * (E // 2))

            overflow(dve, more)


def combine(nc, cst, x3_d, y_d, wts, dest, g, out):
    with ExitStack() as ctx:
        s_ = Scope(nc, ctx, "cb")
        xr = s_.sb("xr", [P, 2, D])
        ys = s_.sb("ys", [P, 2, 2, D])
        ix = s_.sb("ix", [P, 2, 2], I32)
        idle = s_.sb("idle", [1, 8])
        idle_set = s_.sem("idle_set")
        sq = s_.sb("sq", [P, D])
        yo = s_.sb("yo", [P, 2, D])
        gb = s_.sb("gb", [P, D])
        st = s_.sb("st", [P, 2, 3])
        eps = s_.sb("eps", [P, 1])
        x_in, stored = ([s_.sem(f"{n}{i}") for i in range(2)] for n in ("x_in", "stored"))
        y_in = [s_.kept("y_in0"), s_.kept("y_in1")]
        g_in, eps_set, ixd, added, sq_done, rms_done, rcp_done, done = (s_.sem(n) for n in (
            "g_in", "eps_set", "ixd", "added", "sq_done", "rms_done", "rcp_done", "done"))
        block = ctx.enter_context(nc.Block())

        @block.sync
        def _(sp):
            sp.dma_start(gb[:], g.broadcast_to([P, D])).then_inc(g_in, 16)

            def load(i, s):
                sp.dma_start(xr[:, s, :], x3_d[bass.ts(i, P), :]).then_inc(x_in[s], 16)

            def store(i, s):
                sp.wait_ge(done, i + 1)
                sp.dma_start(out[bass.ts(i, P), :], yo[:, s, :]).then_inc(stored[s], 16)

            load(0, 0)
            load(1, 1)
            with sp.Fori(0, NT // 2 - 1) as t:
                for s in range(2):
                    store(2 * t + s, s)
                    load(2 * t + (s + 2), s)
            store(NT - 2, 0)
            store(NT - 1, 1)
            for s in range(2):
                sp.wait_ge(stored[s], 16 * (NT // 2))

        @block.gpsimd
        def _(pool):
            def gather(i, s, first=False):
                if not first:
                    pool.wait_ge(added, 2 * i - 2)
                for a in range(2):
                    nc.gpsimd.tensor_copy(ix[:, s, a:a + 1], dest[:, a, bass.ds(i, 1)]).then_inc(ixd, 1)
                pool.wait_ge(ixd, 2 * i + 2)
                nc.gpsimd.tensor_tensor(idle[:], idle[:], idle[:], ALU.add)
                for a in range(2):
                    nc.gpsimd.indirect_dma_start(ys[:, s, a, :], None, y_d, bass.IndirectOffsetOnAxis(ap=ix[:, s, a:a + 1].bitcast(U32), axis=0)).then_inc(y_in[s], 16)

            nc.gpsimd.memset(idle[:], 0.0).then_inc(idle_set, 1)
            pool.wait_ge(idle_set, 1)
            gather(0, 0, True)
            gather(1, 1, True)
            with pool.Fori(1, NT // 2) as t:
                for s in range(2):
                    gather(2 * t + s, s)

        @block.vector
        def _(dve):
            V = nc.vector
            V.memset(eps[:], EPS).then_inc(eps_set, 1)
            dve.wait_ge(g_in, 16)

            def add(i, s, n):
                dve.wait_ge(x_in[s], n)
                dve.wait_ge(y_in[s], 2 * n)
                for a in range(2):
                    w = wts[:, bass.ds(i, 1), a]
                    V.scalar_tensor_tensor(xr[:, s, :], ys[:, s, a, :], w, xr[:, s, :], ALU.mult, ALU.add).then_inc(added, 1)
                    dve.wait_ge(added, 2 * i + (a + 1))

            def norm(i, s, n):
                dve.wait_ge(rms_done, i + 1)
                V.reciprocal(st[:, s, 2:3], st[:, s, 1:2]).then_inc(rcp_done, 1)
                dve.wait_ge(rcp_done, i + 1)
                dve.wait_ge(stored[s], n)
                V.scalar_tensor_tensor(yo[:, s, :], xr[:, s, :], st[:, s, 2:3], gb[:], ALU.mult, ALU.mult).then_inc(done, 1)

            add(0, 0, 16)
            with dve.Fori(0, NT // 2 - 1) as t:
                add(2 * t + 1, 1, 16 * t + 16)
                norm(2 * t, 0, 16 * t)
                add(2 * t + 2, 0, 16 * t + 32)
                norm(2 * t + 1, 1, 16 * t)
            add(NT - 1, 1, 16 * (NT // 2))
            norm(NT - 2, 0, 16 * (NT // 2 - 1))
            norm(NT - 1, 1, 16 * (NT // 2 - 1))

        @block.scalar
        def _(act):
            act.wait_ge(eps_set, 1)
            with act.Fori(0, NT // 2) as t:
                for s in range(2):
                    i = 2 * t + s
                    act.wait_ge(added, 2 * i + 2)
                    nc.scalar.activation(sq[:], xr[:, s, :], ACT.Square, accum_out=st[:, s, 0:1]).then_inc(sq_done, 1)
                    act.wait_ge(sq_done, i + 1)
                    nc.scalar.activation(st[:, s, 1:2], st[:, s, 0:1], ACT.Sqrt, bias=eps[:], scale=1.0 / D).then_inc(rms_done, 1)


def program(nc, a, out):
    def scratch(name, shape, dt=F32):
        return nc.dram_tensor(name, shape, dt).ap()

    gates_d = scratch("gates_d", (2 * D, T))
    conv_d = scratch("conv_d", (CW, T))
    qn_d, qr_d = scratch("qn_d", (H * NOPE, T)), scratch("qr_d", (H * ROPE, T))
    kn_d, kr_d = scratch("kn_d", (H * NOPE, T)), scratch("kr_d", (ROPE, T))
    v_d = scratch("v_d", (T, H * VD))
    o_d, l_d = scratch("o_d", (H * VD, T)), scratch("l_d", (H, T))
    x2_d, x3_d, h_d = scratch("x2_d", (T, D)), scratch("x3_d", (T, D)), scratch("h_d", (T, D))
    tab_d = scratch("tab_d", (P * 96, 1), I32)
    y_d = scratch("y_d", (NB * P, D))
    x = a["x"]
    with ExitStack() as outer:
        g_ = Scope(nc, outer, "all")
        cst = g_.sb("cst", [P, C_END])
        vec = g_.sb("vec", [P, V_END])
        c_in = g_.sem("c_in")
        with nc.Block() as block:
            @block.sync
            def _(sp):
                sp.dma_start(cst[:], a["consts"]).then_inc(c_in, 16)
                sp.dma_start(vec[:], a["vecs"]).then_inc(c_in, 16)
                sp.wait_ge(c_in, 32)
        with ExitStack() as front:
            f_ = Scope(nc, front, "fr")
            cqT = f_.sb("cqT", [P, 2, T])
            ckvT = f_.sb("ckvT", [P, T])
            krT = f_.sb("krT", [2 * ROPE, T])
            cosT = f_.sb("cosT", [P, T])
            sinT = f_.sb("sinT", [P, T])
            with nc.sbuf_tensor("hT1", [P, KD, T], F32) as hT:
                norm_transpose(nc, "n1", cst, x, a["g_mix"], hT, NT)
                project(nc, cst, vec, hT, a["w_in"], a["w_kr"], a["positions"], gates_d, conv_d, cqT, ckvT, krT, cosT, sinT)
            latents(nc, cst, vec, cqT, ckvT, krT, cosT, sinT, a["w_uq"], a["w_uk"], a["w_uv"], qn_d, qr_d, kn_d, kr_d, v_d)
        attention(nc, cst, qn_d, qr_d, kn_d, kr_d, v_d, o_d, l_d)
        mix(nc, cst, o_d, l_d, conv_d, gates_d, x, a["w_branch_a"], a["w_branch_b"], a["w_out"], x2_d)
        with ExitStack() as mid:
            m_ = Scope(nc, mid, "mi")
            kmT = m_.sb("kmT", [P, XH, MEM])
            vm = m_.sb("vm", [P, MEM // P, XH * XD])
            with nc.sbuf_tensor("memT", [P, KD, MEM], F32) as memT:
                norm_transpose(nc, "nm", cst, a["mem"], a["g_mem"], memT, MEM // P)
                mem_keys_values(nc, memT, a["w_kv_mem"], kmT, vm)
            with nc.sbuf_tensor("hT2", [P, KD, T], F32) as hT:
                norm_transpose(nc, "n2", cst, x2_d, a["g_xattn"], hT, NT)
                cross_attention(nc, cst, hT, kmT, vm, a["w_q_mem"], a["w_o_mem"], x2_d, x3_d, y_d)
        clear_semaphores(nc)
        with ExitStack() as back:
            b_ = Scope(nc, back, "ba")
            wts = b_.sb("wts", [P, NT, 2])
            dest = b_.sb("dest", [P, 2, NT], I32)
            tab = b_.sb("tab", [P, 96], I32)
            meta = b_.sb("meta", [1, 40], I32)
            with nc.sbuf_tensor("hT3", [P, KD, T], F32) as hT:
                norm_transpose(nc, "n3", cst, x3_d, a["g_moe"], hT, NT, h_d)
                route(nc, cst, hT, a["w_r"], a["b_r"], tab_d, wts, dest, tab, meta)
            experts(nc, cst, h_d, a["w_gate_up"], a["w_down"], y_d, tab, meta)
            combine(nc, cst, x3_d, y_d, wts, dest, a["g_final"], out)


def constants():
    c = np.zeros((P, C_END), np.float32)
    p = np.arange(P)
    c[:, C_ID:C_ID + P] = np.eye(P)
    c[:, C_NEG:C_NEG + P] = np.where(p[None, :] > p[:, None], NEG, 0.0)
    c[:, C_LT:C_LT + P] = p[:, None] < p[None, :]
    c[:, C_IOTA:C_IOTA + 64] = np.arange(64)
    c[:, C_INV] = (10000.0 ** (-np.arange(0, ROPE, 2) / ROPE))[p % 16]
    c[:, C_SGN] = np.where(p % 32 < 16, -1.0, 1.0)
    c[:, C_NEGT:C_NEGT + P] = np.where(p[:, None] > p[None, :], NEG, 0.0)
    c[:, C_ONE] = 1.0
    c[:, C_E128:C_E128 + E] = P * np.arange(E)
    return c


def kernel(**inputs):
    import concourse.bacc as bacc
    from concourse.bass_utils import run_bass_kernel_spmd

    w = {n: np.asarray(v) for n, v in inputs.items()}
    w_in = w["w_in"][0]
    LQ, LKV = w["g_cq"].shape[1], w["g_ckv"].shape[1]
    kr = w_in[:, LQ + LKV:LQ + LKV + ROPE]
    swap = np.r_[ROPE // 2:ROPE, 0:ROPE // 2]
    uq = w["w_uq"][0].reshape(LQ, H, QKD)
    ukv = w["w_ukv"][0].reshape(LKV, H, NOPE + VD)
    cols = lambda v: v.reshape(-1, P).T
    arrays = {
        "x": w["x"][0], "mem": w["mem"][0], "positions": w["positions"],
        "g_mix": w["g_mix"], "g_xattn": w["g_xattn"], "g_mem": w["g_mem"], "g_moe": w["g_moe"], "g_final": w["g_final"].reshape(1, D),
        "w_in": w_in, "w_kr": np.concatenate([kr, kr[:, swap]], 1),
        "w_uq": np.concatenate([uq[:, :, :NOPE].reshape(LQ, -1), uq[:, :, NOPE:].reshape(LQ, -1), uq[:, :, NOPE:][:, :, swap].reshape(LQ, -1)], 1),
        "w_uk": ukv[:, :, :NOPE].reshape(LKV, -1), "w_uv": ukv[:, :, NOPE:].reshape(LKV, -1),
        "w_branch_a": w["w_branch_a"][0], "w_branch_b": w["w_branch_b"][0], "w_out": w["w_out"][0],
        "w_q_mem": w["w_q_mem"][0], "w_kv_mem": w["w_kv_mem"][0], "w_o_mem": w["w_o_mem"][0],
        "w_r": np.concatenate([w["w_router_group"][0], w["w_router_expert"][0]], 1),
        "b_r": np.concatenate([w["b_router_group"], w["b_router_expert"]], 1),
        "w_gate_up": w["w_gate_up"][0], "w_down": w["w_down"][0],
        "vecs": np.concatenate([w["conv_w"][0].T.reshape(CW // P, P, 3).transpose(1, 0, 2).reshape(P, -1),
                                cols(w["b_gate"][0]), cols(w["g_cq"][0]), cols(w["g_ckv"][0])], 1),
        "consts": constants(),
    }
    nc = bacc.Bacc("TRN2", target_bir_lowering=False, num_devices=1)
    feed, aps = {}, {}
    for name, v in arrays.items():
        v = np.ascontiguousarray(v)
        feed[f"in_{name}"] = v
        aps[name] = nc.dram_tensor(f"in_{name}", v.shape, mybir.dt.from_np(v.dtype), kind="ExternalInput").ap()
    out = nc.dram_tensor("out", (T, D), F32, kind="ExternalOutput").ap()
    program(nc, aps, out)
    r = run_bass_kernel_spmd(nc, [feed], core_ids=[0])
    return r.results[0]["out"].reshape(1, T, D)
```

```python
import math
from contextlib import ExitStack

import numpy as np
import concourse.bass as bass
from concourse import mybir

P = 128
D = 1024
KD = D // P
T = 2048
NT = T // P
CH = 512
NC_ = T // CH
TH = T // 2
MEM = 256
H = 8
NOPE, ROPE, VD = 64, 32, 64
QKD = NOPE + ROPE
CW = 512
XH, XD = 4, 128
G, EG = 8, 8
E = G * EG
FF = 256
OVF = T * 2 // P - 1
NB = E + OVF + 1
EPS = 1e-6
NEG = -1e30
TWO_PI_PARTS = (6.28125, 0.00193500518798828125, 3.01991612900e-07)

PI_IN = 3.1415925

ALU = mybir.AluOpType
ACT = mybir.ActivationFunctionType
F32 = mybir.dt.float32
F32R = mybir.dt.float32r
BF16 = mybir.dt.bfloat16
I32 = mybir.dt.int32
U32 = mybir.dt.uint32
AX = mybir.AxisListType.X

C_ID, C_NEG, C_LT, C_IOTA, C_INV, C_SGN, C_E128, C_NEGT, C_ONE, C_END = 0, 128, 256, 384, 448, 449, 450, 514, 642, 645
V_CONV, V_BG, V_CQ, V_CKV, V_END = 0, 12, 28, 30, 31


class Scope:

    def __init__(self, nc, ctx, tag):
        self.nc, self.ctx, self.tag = nc, ctx, tag

    def sb(self, name, shape, dt=F32):
        return self.ctx.enter_context(self.nc.sbuf_tensor(f"{self.tag}_{name}", shape, dt))

    def ps(self, name, shape, dt=F32):
        return self.ctx.enter_context(self.nc.psum_tensor(f"{self.tag}_{name}", shape, dt))

    def sem(self, name):
        return self.ctx.enter_context(self.nc.semaphore(f"{self.tag}_{name}"))

    def kept(self, name):
        return self.nc.alloc_semaphore(f"{self.tag}_{name}")


def clear_semaphores(nc):
    used = sorted(nc.released_uncleared_semaphores)
    with nc.Block() as block:
        @block.gpsimd
        def _(pool):
            runs = []
            for n in used:
                if runs and runs[-1][1] == n:
                    runs[-1][1] = n + 1
                else:
                    runs.append([n, n + 1])
            for a, b in runs:
                pool.sem_clear(range(a, b))


def norm_transpose(nc, tag, cst, src, g, hT, nt, rows_out=None, low=None, ask=None):
    R = min(4, nt)
    with ExitStack() as ctx:
        s_ = Scope(nc, ctx, tag)
        xr = s_.sb("xr", [P, R, D])
        xn = s_.sb("xn", [P, 2, D])
        sq = s_.sb("sq", [P, D])
        gb = s_.sb("gb", [P, D])
        st = s_.sb("st", [P, R, 3])
        eps = s_.sb("eps", [P, 1])
        tp = [s_.ps(f"tp{i}", [P, 4, P]) for i in range(4)]
        x_in = [s_.sem(f"x_in{i}") for i in range(R)]
        g_in, eps_set, sq_done, rms_done = s_.sem("g_in"), s_.sem("eps_set"), s_.sem("sq_done"), s_.sem("rms_done")
        rcp_done, norm_done, turned = s_.sem("rcp_done"), s_.sem("norm_done"), s_.sem("turned")
        out_a, out_v, out_hi = s_.sem("out_a"), s_.sem("out_v"), s_.sem("out_hi")
        stored = [s_.sem("stored0"), s_.sem("stored1")]
        ident = cst[:, C_ID:C_ID + P]
        block = ctx.enter_context(nc.Block())

        def tiles(eng, step, ahead):
            start, n = ahead
            for s in range(min(n, nt)):
                start(0, s)
            if nt > R:
                with eng.Fori(0, nt // R - 1) as t:
                    for s in range(R):
                        step(t, s)
                        start(t, s + n)
            for s in range(R):
                step(nt // R - 1, s)
                if s + n < R:
                    start(nt // R - 1, s + n)

        @block.sync
        def _(sp):
            def load(t, s):
                if not isinstance(t, int) or t > 0 or s >= R:
                    sp.wait_ge(norm_done, R * t + (s - R + 1))
                sp.dma_start(xr[:, s % R, :], src[bass.ds(P * R * t + P * s, P), :]).then_inc(x_in[s % R], 16)

            def store(t, s):
                if rows_out is not None:
                    sp.wait_ge(norm_done, R * t + (s + 1))
                    sp.dma_start(rows_out[bass.ds(P * R * t + P * s, P), :], xn[:, s % 2, :]).then_inc(stored[s % 2], 16)

            for e in range(2):
                sp.sem_inc(stored[e], 16)
            load(0, 0)
            sp.dma_start(gb[:], g.broadcast_to([P, D])).then_inc(g_in, 16)
            for s in range(1, R):
                load(0, s)
            if ask is not None:
                ask(sp)
            if nt > R:
                with sp.Fori(0, nt // R - 1) as t:
                    for s in range(R):
                        store(t, s)
                        load(t, s + R)
            for s in range(R):
                store(nt // R - 1, s)
            if rows_out is not None:
                for e in range(2):
                    sp.wait_ge(stored[e], 16 * (nt // 2) + 16)

        @block.scalar
        def _(act):
            act.wait_ge(eps_set, 1)

            def squares(t, s):
                act.wait_ge(x_in[s % R], 16 * t + 16 * (s // R + 1))
                nc.scalar.activation(sq[:], xr[:, s % R, :], ACT.Square, accum_out=st[:, s % R, 0:1]).then_inc(sq_done, 1)
                act.wait_ge(sq_done, R * t + (s + 1))
                nc.scalar.activation(st[:, s % R, 1:2], st[:, s % R, 0:1], ACT.Sqrt, bias=eps[:], scale=1.0 / D).then_inc(rms_done, 1)

            def copy_out(t, s):
                tile = bass.ds(P * R * t + P * s, P)
                act.wait_ge(turned, R * t + (s + 1))
                if low is not None:
                    nc.scalar.copy(hT[:, 4:8, tile], tp[2 * (s % 2) + 1][:]).then_inc(out_hi, 1)
                nc.scalar.copy(hT[:, 0:4, tile], tp[2 * (s % 2)][:]).then_inc(out_a, 1)

            tiles(act, copy_out, (squares, 3))

        @block.vector
        def _(dve):
            dve.sem_inc(out_v, 2)
            nc.vector.memset(eps[:], EPS).then_inc(eps_set, 1)
            dve.wait_ge(g_in, 16)

            def norm(t, s):
                dve.wait_ge(rms_done, R * t + (s + 1))
                nc.vector.reciprocal(st[:, s % R, 2:3], st[:, s % R, 1:2]).then_inc(rcp_done, 1)
                dve.wait_ge(rcp_done, R * t + (s + 1))
                if not isinstance(t, int) or t > 0 or s >= 2:
                    dve.wait_ge(turned, R * t + (s - 1))
                if rows_out is not None:
                    dve.wait_ge(stored[s % 2], 16 * (R // 2) * t + 16 * (s // 2 + 1))
                nc.vector.scalar_tensor_tensor(xn[:, s % 2, :], xr[:, s % R, :], st[:, s % R, 2:3], gb[:], ALU.mult, ALU.mult).then_inc(norm_done, 1)

            def copy_out(t, s):
                tile, b = bass.ds(P * R * t + P * s, P), 2 * (s % 2)
                if low is None:
                    dve.wait_ge(turned, R * t + (s + 1))
                    nc.vector.tensor_copy(hT[:, 4:8, tile], tp[b + 1][:]).then_inc(out_v, 1)
                    return
                for half, ready in ((1, out_hi), (0, out_a)):
                    dve.wait_ge(ready, R * t + (s + 1))
                    f = slice(4 * half, 4 * half + 4)
                    ins = nc.vector.tensor_tensor(low[:, f, tile], tp[b + half][:], hT[:, f, tile], ALU.subtract)
                ins.then_inc(out_v, 1)

            tiles(dve, copy_out, (norm, 2))

        @block.tensor
        def _(pe):
            if low is None:
                pe.sem_inc(out_a, 2)

            def turn(t, s):
                pe.wait_ge(norm_done, R * t + (s + 1))
                pe.wait_ge(out_v, R * t + (s + 1))
                if low is None:
                    pe.wait_ge(out_a, R * t + (s + 1))
                for k in range(KD):
                    mm = nc.tensor.transpose(tp[2 * (s % 2) + k // 4][:, k % 4, :], xn[:, s % 2, k * P:(k + 1) * P], ident)
                mm.then_inc(turned, 1)

            tiles(pe, turn, (lambda t, s: None, 0))


def project(nc, tag, cst, vec, hh, hl, w_slabs, pos, t0, halo, gates_d, conv_d, cqT, ckvT, krT, cosT, sinT):
    with ExitStack() as ctx:
        s_ = Scope(nc, ctx, tag)
        raw = s_.sb("raw", [P, 2, KD, P])
        wh = s_.sb("wh", [P, 2, KD, P], F32R)
        wl = s_.sb("wl", [P, 2, KD, P], F32R)
        gst = s_.sb("gst", [P, 2, TH])
        bcx = s_.sb("bcx", [P, 3, TH])
        u = s_.sb("u", [P, TH + 2])
        y = s_.sb("y", [P, TH])
        bias = s_.sb("bias", [P, 2])
        NCH = TH // CH
        acc = [s_.ps(f"acc{i}", [P, CH]) for i in range(2 * NCH)]
        w_ready = [s_.sem("w0"), s_.sem("w1")]
        bias_set, w_hi, w_lo, mm_done, evac, y_done, y_out = (s_.sem(n) for n in ("bias_set", "w_hi", "w_lo", "mm", "evac", "y_done", "y_out"))
        angle_step, conv_step, pos_in = s_.sem("angle_step"), s_.sem("conv_step"), s_.sem("pos_in")
        g_out = [s_.sem("g_out0"), s_.sem("g_out1")]
        LAT, CONV, GATE = 4, 3 * CW // P, 2 * D // P
        N = LAT + CONV + GATE
        here = slice(t0, t0 + TH)
        posi = gst[:, 0, :].bitcast(I32)
        block = ctx.enter_context(nc.Block())

        @block.sync
        def _(sp):
            def load(n, s):
                sp.dma_start(raw[:, s], w_slabs[bass.ds(n, 1)].rearrange("a p k n -> p (a k) n")).then_inc(w_ready[s], 16)

            def next_load(n, s):
                sp.wait_ge(w_lo, n + 1)
                load(n + 2, s)

            def store_gates(g, s):
                sp.wait_ge(evac, NCH * (g + LAT + CONV + 1))
                sp.dma_start(gates_d[bass.ds(g * P, P), here], gst[:, s, :]).then_inc(g_out[s], 16)

            sp.dma_start(posi, pos[:, here].broadcast_to([P, TH])).then_inc(pos_in, 16)
            sp.sem_inc(y_out, 16)
            for s in range(2):
                sp.sem_inc(g_out[s], 16)
                load(s, s)
            for n in range(LAT):
                next_load(n, n % 2)
            with sp.Fori(0, CW // P // 2) as t:
                for q in range(6):
                    next_load(6 * t + (q + LAT), q % 2)
                    if q % 3 == 2:
                        sp.wait_ge(y_done, 2 * t + (q // 3 + 2))
                        sp.dma_start(conv_d[bass.ds((2 * t + q // 3) * P, P), here], y[:]).then_inc(y_out, 16)
            with sp.Fori(0, GATE // 2 - 1) as t:
                for s in range(2):
                    next_load(2 * t + (s + LAT + CONV), s)
                    store_gates(2 * t + s, s)
            for s in range(2):
                store_gates(GATE - 2 + s, s)
            sp.wait_ge(y_out, 16 * (CW // P + 1))
            for s in range(2):
                sp.wait_ge(g_out[s], 16 * (GATE // 2 + 1))

        @block.tensor
        def _(pe):
            def run(n, s, again):
                pe.wait_ge(w_lo, n + 1)
                for c in range(NCH):
                    if again:
                        pe.wait_ge(evac, NCH * n + (c + 1 - 2 * NCH))
                    t = slice(c * CH, (c + 1) * CH)
                    for i, (w, h) in enumerate(((wh, hh), (wl, hh), (wh, hl))):
                        for k in range(KD):
                            mm = nc.tensor.matmul(acc[NCH * s + c][:], w[:, s, k, :], h[:, k, t],
                                                  start=(i == 0 and k == 0), stop=(i == 2 and k == KD - 1))
                    mm.then_inc(mm_done, 1)

            for n in range(2):
                run(n, n, False)
            with pe.Fori(1, N // 2) as t:
                for s in range(2):
                    run(2 * t + s, s, True)

        @block.scalar
        def _(act):
            def high(n, s, n_w, again=True):
                act.wait_ge(w_ready[s], n_w)
                if again:
                    act.wait_ge(mm_done, NCH * (n - 1))
                nc.scalar.copy(wh[:, s], raw[:, s]).then_inc(w_hi, 1)

            def take(n, s, dst, m=P, bias=None):
                for c in range(NCH):
                    act.wait_ge(mm_done, NCH * n + c + 1)
                    o, i = dst[:, c * CH:(c + 1) * CH], acc[NCH * s + c][0:m, :]
                    if bias is None:
                        nc.scalar.copy(o, i).then_inc(evac, 1)
                    else:
                        nc.scalar.activation(o, i, ACT.Sigmoid, bias=bias).then_inc(evac, 1)

            high(0, 0, 16, False)
            for n, dst, m in ((0, cqT[:, 0, here], P), (1, cqT[:, 1, here], P), (2, ckvT[:, here], P), (3, krT[0:2 * ROPE, here], 2 * ROPE)):
                high(n + 1, (n + 1) % 2, 16 * ((n + 1) // 2 + 1), n > 0)
                take(n, n % 2, dst, m)
            with act.Fori(0, CW // P // 2) as t:
                for q in range(6):
                    high(6 * t + (q + LAT + 1), (q + 1) % 2, 48 * t + 16 * ((q + LAT + 1) // 2 + 1))
                    if q % 3 == 0:
                        act.wait_ge(y_done, 2 * t + (q // 3 + 1))
                    take(6 * t + (q + LAT), q % 2, bcx[:, q % 3, :])

            def gate(g, s):
                nc.scalar.copy(bias[:, s:s + 1], vec[:, bass.ds(g + V_BG, 1)]).then_inc(bias_set, 1)
                act.wait_ge(bias_set, g + 1)
                act.wait_ge(g_out[s], 8 * (g - s) + 16)
                take(g + LAT + CONV, s, gst[:, s, :], P, bias[:, s:s + 1])

            act.wait_ge(angle_step, 1)
            with act.Fori(0, GATE // 2 - 1) as t:
                high(2 * t + (LAT + CONV + 1), 1, 16 * t + 16 * ((LAT + CONV) // 2 + 1))
                gate(2 * t, 0)
                high(2 * t + (LAT + CONV + 2), 0, 16 * t + 16 * ((LAT + CONV) // 2 + 2))
                gate(2 * t + 1, 1)
            high(N - 1, 1, 16 * (N // 2))
            gate(GATE - 2, 0)
            gate(GATE - 1, 1)

        @block.vector
        def _(dve):
            V = nc.vector
            done = [0]

            def link(ins):
                done[0] += 1
                ins.then_inc(angle_step, 1)
                dve.wait_ge(angle_step, done[0])

            def low(n, s):
                dve.wait_ge(w_hi, n + 1)
                V.tensor_tensor(wl[:, s], raw[:, s], wh[:, s], ALU.subtract).then_inc(w_lo, 1)

            dve.sem_inc(y_done, 1)
            low(0, 0)
            low(1, 1)
            dve.wait_ge(pos_in, 16)
            link(V.tensor_copy(y[:], posi))
            sin, cos = sinT[:, here], cosT[:, here]
            link(V.tensor_scalar(sin, y[:], cst[:, C_INV:C_INV + 1], None, ALU.mult))
            link(V.tensor_scalar(y[:], sin, 1.0 / (2 * math.pi), 12582912.0, ALU.mult, ALU.add))
            link(V.tensor_scalar(y[:], y[:], 12582912.0, None, ALU.subtract))
            for part in TWO_PI_PARTS:
                link(V.scalar_tensor_tensor(sin, y[:], -part, sin, ALU.mult, ALU.add))
            link(V.tensor_scalar(cos, sin, math.pi / 2, None, ALU.add))
            link(V.tensor_scalar(y[:], cos, math.pi, -2 * math.pi, ALU.is_gt, ALU.mult))
            link(V.tensor_tensor(cos, cos, y[:], ALU.add))
            for tab in (cos, sin):
                link(V.tensor_scalar(tab, tab, PI_IN, -PI_IN, ALU.min, ALU.max))
            if t0 == 0:
                link(V.memset(halo[:], 0.0))
            for n in range(2, LAT + 1):
                low(n, n % 2)

            def conv(j):
                def step(ins, n):
                    ins.then_inc(conv_step, 1)
                    dve.wait_ge(conv_step, 6 * j + n)

                dve.wait_ge(evac, 3 * NCH * j + NCH * (LAT + 3))
                b, c, x = (bcx[:, r, :] for r in range(3))
                wc = [vec[:, bass.ds(3 * j + (r + V_CONV), 1)] for r in range(3)]
                one = cst[:, C_ONE:C_ONE + 1]
                V.tensor_scalar(u[:, 0:2], halo[:, bass.ds(2 * j, 2)], one, None, ALU.mult).then_inc(conv_step, 1)
                step(V.tensor_tensor(u[:, 2:TH + 2], c, x, ALU.mult), 2)
                V.tensor_scalar(halo[:, bass.ds(2 * j, 2)], u[:, TH:TH + 2], one, None, ALU.mult).then_inc(conv_step, 1)
                dve.wait_ge(y_out, 16 * j + 16)
                step(V.tensor_scalar(y[:], u[:, 0:TH], wc[0], None, ALU.mult), 4)
                for r in (1, 2):
                    step(V.scalar_tensor_tensor(y[:], u[:, r:TH + r], wc[r], y[:], ALU.mult, ALU.add), 4 + r)
                V.tensor_tensor(y[:], y[:], b, ALU.mult).then_inc(y_done, 1)

            with dve.Fori(0, CW // P // 2) as t:
                for q in range(6):
                    low(6 * t + (q + LAT + 1), (q + 1) % 2)
                    if q % 3 == 2:
                        conv(2 * t + q // 3)
            with dve.Fori(0, GATE // 2 - 1) as t:
                for s in (1, 0):
                    low(2 * t + (LAT + CONV + 2 - s), s)
            low(N - 1, 1)


def latents(nc, cst, vec, cqT, ckvT, krT, cosT, sinT, w_uq, w_uk, w_uv, qn_d, qr_d, kn_d, kr_d, v_d):
    QS = 1.0 / math.sqrt(QKD)
    with ExitStack() as ctx:
        s_ = Scope(nc, ctx, "lt")
        wq = s_.sb("wq", [P, 2, 8 * P])
        wk = s_.sb("wk", [P, 4 * P])
        wv = s_.sb("wv", [P, 4 * P])
        ones = s_.sb("ones", [P, P])
        eps = s_.sb("eps", [P, 1])
        sq = s_.sb("sq", [P, 3, CH])
        rs = s_.sb("rs", [P, 2, CH])
        cn = s_.sb("cn", [P, 3, CH])
        qn = s_.sb("qn", [P, 4, CH])
        kn = s_.sb("kn", [P, 4, CH])
        vv = s_.sb("vv", [P, 4, CH])
        ra = s_.sb("ra", [P, 2, CH])
        rb = s_.sb("rb", [P, 2, CH])
        ka = s_.sb("ka", [ROPE, CH])
        kb = s_.sb("kb", [ROPE, CH])
        psS = [s_.ps(f"psS{i}", [P, CH]) for i in range(2)]
        psR = [s_.ps(f"psR{i}", [P, CH]) for i in range(4)]
        psU = [s_.ps(f"psU{i}", [P, CH]) for i in range(2)]
        w_in, set_, tab, squared, stat, rooted = (s_.sem(n) for n in ("w_in", "set", "tab", "squared", "stat", "rooted"))
        rcp, q_normed, kv_normed, rope_mm, unit_mm, taken = (s_.sem(n) for n in ("rcp", "q_normed", "kv_normed", "rope_mm", "unit_mm", "taken"))
        rot, rot_done, stored = s_.sem("rot"), s_.sem("rot_done"), s_.sem("stored")
        block = ctx.enter_context(nc.Block())
        NST = 5

        @block.sync
        def _(sp):
            sp.dma_start(wq[:], w_uq.rearrange("(k p) n -> p k n", p=P)).then_inc(w_in, 16)
            sp.dma_start(wk[:], w_uk).then_inc(w_in, 16)
            sp.dma_start(wv[:], w_uv).then_inc(w_in, 16)
            sp.sem_inc(stored, 16 * NST)
            with sp.Fori(0, NC_) as c:
                t = bass.ts(c, CH)
                sp.wait_ge(rot_done, c + 2)
                sp.dma_start(qr_d[:, t].rearrange("(j p) n -> p j n", p=P), ra[:]).then_inc(stored, 16)
                sp.dma_start(kr_d[:, t], ka[:]).then_inc(stored, 16)
                sp.wait_ge(taken, 12 * c + 6)
                sp.dma_start(qn_d[:, t].rearrange("(j p) n -> p j n", p=P), qn[:]).then_inc(stored, 16)
                sp.wait_ge(taken, 12 * c + 10)
                sp.dma_start(kn_d[:, t].rearrange("(j p) n -> p j n", p=P), kn[:]).then_inc(stored, 16)
                sp.wait_ge(taken, 12 * c + 14)
                sp.dma_start(v_d[t, :].rearrange("(j p) n -> p j n", p=P), vv[:]).then_inc(stored, 16)
            sp.wait_ge(stored, 16 * NST * NC_ + 16 * NST)

        def chunks(eng, run):
            with eng.Fori(0, NC_ - 1) as c:
                run(c, True)
            run(NC_ - 1, False)

        @block.scalar
        def _(act):
            def squares(c):
                t = bass.ts(c, CH)
                nc.scalar.activation(sq[:, 0:2, :], cqT[:, :, t], ACT.Square).then_inc(squared, 1)
                nc.scalar.activation(sq[:, 2, :], ckvT[:, t], ACT.Square).then_inc(squared, 1)

            def roots(c):
                for i, n in enumerate((2 * P, P)):
                    act.wait_ge(stat, 2 * c + i + 1)
                    nc.scalar.activation(rs[:, i, :], psS[i][:], ACT.Sqrt, bias=eps[:], scale=1.0 / n).then_inc(rooted, 1)

            act.sem_inc(taken, 2)
            act.wait_ge(set_, 2)
            squares(0)
            roots(0)
            for x in (sinT, cosT):
                nc.scalar.activation(x[:], x[:], ACT.Sin).then_inc(tab, 1)

            def chunk(c, more):
                if more:
                    squares(c + 1)
                act.wait_ge(stored, 16 * NST * c + 16 * NST)
                for u in range(12):
                    act.wait_ge(unit_mm, 12 * c + u + 1)
                    dst = (qn, kn, vv)[u // 4][:, u % 4, :]
                    nc.scalar.activation(dst, psU[u % 2][:], ACT.Copy, scale=QS if u < 4 else 1.0).then_inc(taken, 1)
                    if more and u == 4:
                        act.wait_ge(kv_normed, c + 1)
                        roots(c + 1)

            chunks(act, chunk)

        @block.vector
        def _(dve):
            V = nc.vector

            def inverses(c):
                for i in range(2):
                    dve.wait_ge(rooted, 2 * c + i + 1)
                    V.reciprocal(rs[:, i, :], rs[:, i, :]).then_inc(rcp, 1)
                dve.wait_ge(rcp, 2 * c + 2)

            def norm(c, i):
                x = cqT[:, i, bass.ts(c, CH)] if i < 2 else ckvT[:, bass.ts(c, CH)]
                V.scalar_tensor_tensor(cn[:, i, :], x, vec[:, V_CQ + i:V_CQ + i + 1], rs[:, i // 2, :],
                                       ALU.mult, ALU.mult).then_inc(q_normed if i < 2 else kv_normed, 1)

            V.memset(ones[:], 1.0).then_inc(set_, 1)
            V.memset(eps[:], EPS).then_inc(set_, 1)
            dve.sem_inc(rot_done, 1)
            inverses(0)
            for i in range(3):
                norm(0, i)
            dve.wait_ge(tab, 2)
            V.tensor_scalar(sinT[:], sinT[:], cst[:, C_SGN:C_SGN + 1], None, ALU.mult).then_inc(tab, 1)
            dve.wait_ge(tab, 3)

            def chunk(c, more):
                t = bass.ts(c, CH)
                dve.wait_ge(stored, 16 * NST * c + 16 * NST)
                V.tensor_tensor(ka[:], krT[0:ROPE, t], cosT[0:ROPE, t], ALU.mult).then_inc(rot, 1)
                V.tensor_tensor(kb[:], krT[ROPE:2 * ROPE, t], sinT[ROPE:2 * ROPE, t], ALU.mult).then_inc(rot, 1)
                for i in range(4):
                    dve.wait_ge(rope_mm, 4 * c + i + 1)
                    dst, tabl = ((ra, cosT), (rb, sinT))[i % 2]
                    V.scalar_tensor_tensor(dst[:, i // 2, :], psR[i][:], QS, tabl[:, t], ALU.mult, ALU.mult).then_inc(rot, 1)
                dve.wait_ge(rot, 7 * c + 6)
                V.tensor_tensor(ka[:], ka[:], kb[:], ALU.add).then_inc(rot, 1)
                dve.wait_ge(rot, 7 * c + 7)
                V.tensor_tensor(ra[:], ra[:], rb[:], ALU.add).then_inc(rot_done, 1)
                if more:
                    inverses(c + 1)
                    dve.wait_ge(unit_mm, 12 * c + 4)
                    for i in range(2):
                        norm(c + 1, i)
                    dve.wait_ge(unit_mm, 12 * c + 12)
                    norm(c + 1, 2)

            chunks(dve, chunk)

        @block.tensor
        def _(pe):
            def sums(c):
                pe.wait_ge(squared, 2 * c + 1)
                nc.tensor.matmul(psS[0][:], ones[:], sq[:, 0, :], start=True, stop=False)
                nc.tensor.matmul(psS[0][:], ones[:], sq[:, 1, :], start=False, stop=True).then_inc(stat, 1)
                pe.wait_ge(squared, 2 * c + 2)
                nc.tensor.matmul(psS[1][:], ones[:], sq[:, 2, :], start=True, stop=True).then_inc(stat, 1)

            pe.wait_ge(set_, 2)
            sums(0)
            pe.wait_ge(w_in, 48)

            def chunk(c, more):
                pe.wait_ge(q_normed, 2 * c + 2)
                pe.wait_ge(rot_done, c + 1)
                for i in range(4):
                    f = (4 + i // 2 + 2 * (i % 2)) * P
                    for k in range(2):
                        mm = nc.tensor.matmul(psR[i][:], wq[:, k, f:f + P], cn[:, k, :], start=(k == 0), stop=(k == 1))
                    mm.then_inc(rope_mm, 1)
                if more:
                    sums(c + 1)
                for u in range(12):
                    pe.wait_ge(taken, 12 * c + u + 1)
                    if u == 4:
                        pe.wait_ge(kv_normed, c + 1)
                    if u < 4:
                        for k in range(2):
                            mm = nc.tensor.matmul(psU[u % 2][:], wq[:, k, u * P:(u + 1) * P], cn[:, k, :], start=(k == 0), stop=(k == 1))
                    elif u < 8:
                        mm = nc.tensor.matmul(psU[u % 2][:], wk[:, (u - 4) * P:(u - 3) * P], cn[:, 2, :], start=True, stop=True)
                    else:
                        mm = nc.tensor.matmul(psU[u % 2][:], cn[:, 2, (u - 8) * P:(u - 7) * P], wv[:], start=True, stop=True)
                    mm.then_inc(unit_mm, 1)

            chunks(pe, chunk)


def attention(nc, cst, qn_d, qr_d, kn_d, kr_d, v_d, o_d, l_d):
    rows = [(i, c) for i in range(NT) for c in range(i // 4 + 1)]
    cols = [(c, j) for c in range(NC_) for j in range(4 * c + 4)]
    NU, NA = len(cols), len(rows) + 1
    RING, AHEAD, PIECES = 4, 3, 2 * NC_ + 1
    A0, A1 = 11, 35
    a_at = {}
    for v in range(NA):
        a_at.setdefault(A0 + v * (A1 - A0) // NA, []).append(v)
    KA, VA = QKD + 2, VD + 2
    with ExitStack() as ctx:
        s_ = Scope(nc, ctx, "at")
        qraw = s_.sb("qraw", [QKD, T])
        kraw = s_.sb("kraw", [QKD, T])
        vraw = s_.sb("vraw", [P, NT, VD])
        qh = s_.sb("qh", [KA, 2, T], F32R)
        ql = s_.sb("ql", [QKD, 2, T], F32R)
        kh = s_.sb("kh", [KA, 2, T], F32R)
        kl = s_.sb("kl", [QKD, 2, T], F32R)
        vh = s_.sb("vh", [P, 2, NT, VA], F32R)
        vl = s_.sb("vl", [P, 2, NT, VA], F32R)
        pf = s_.sb("pf", [P, RING, CH])
        ph = s_.sb("ph", [P, RING, CH], F32R)
        pl = s_.sb("pl", [P, RING, CH], F32R)
        ost = s_.sb("ost", [VA, 2, CH])
        nm = s_.sb("nm", [P, NT, 4])
        mm_ = s_.sb("mm", [P, NT])
        mh = s_.sb("mh", [NT, P], F32R)
        ml = s_.sb("ml", [NT, P], F32R)
        idb = s_.sb("idb", [P, P], BF16)
        neg = s_.sb("neg", [P, P], BF16)
        negT = s_.sb("negT", [P, P], BF16)
        psS = [s_.ps(f"psS{i}", [P, CH]) for i in range(RING)]
        psA = [s_.ps(f"psA{i}", [P, CH]) for i in range(2)]
        psO = [s_.ps(f"psO{i}", [P, CH]) for i in range(2)]
        names = ("raw_in", "set", "split_a", "split_p", "st", "hi", "pv", "o_out", "a_mm", "a_max", "mmin", "mhd", "mld", "m_in")
        raw_in, set_, split_a, split_p, st, hi, pv, o_out, a_mm, a_max, mmin, mhd, mld, m_in = (s_.sem(n) for n in names)
        lo = [s_.sem("lo_even"), s_.sem("lo_odd")]
        o_st = [s_.sem("o_st0"), s_.sem("o_st1")]
        ident = cst[:, C_ID:C_ID + P]
        block = ctx.enter_context(nc.Block())

        def heads(eng, run):
            with eng.Fori(0, H // 2 - 1) as t:
                for s in range(2):
                    run(2 * t + s, s, True)
            run(H - 2, 0, True)
            run(H - 1, 1, False)

        @block.sync
        def _(sp):
            def load(h):
                sp.dma_start(qraw[0:NOPE, :], qn_d[bass.ts(h, NOPE), :]).then_inc(raw_in, 16)
                sp.dma_start(qraw[NOPE:QKD, :], qr_d[bass.ts(h, ROPE), :]).then_inc(raw_in, 16)
                sp.dma_start(kraw[0:NOPE, :], kn_d[bass.ts(h, NOPE), :]).then_inc(raw_in, 16)
                sp.dma_start(kraw[NOPE:QKD, :], kr_d).then_inc(raw_in, 16)
                sp.dma_start(vraw[:], v_d[:, bass.ts(h, VD)].rearrange("(i p) d -> p i d", p=P)).then_inc(raw_in, 16)

            def maxima(h, s):
                sp.wait_ge(mld, h + 1)
                sp.dma_start(qh[QKD:QKD + 1, s, :].bitcast(F32).rearrange("a (i p) -> a i p", p=P), mh[:].bitcast(F32)).then_inc(m_in, 16)
                sp.dma_start(qh[QKD + 1:QKD + 2, s, :].bitcast(F32).rearrange("a (i p) -> a i p", p=P), ml[:].bitcast(F32)).then_inc(m_in, 16)

            def store(h, c):
                sp.wait_ge(o_out, 4 * h + c + 3)
                t = slice(c * CH, (c + 1) * CH)
                sp.dma_start(o_d[bass.ts(h, VD), t], ost[0:VD, c % 2, :]).then_inc(o_st[c % 2], 16)
                sp.dma_start(l_d[bass.ds(h, 1), t], ost[VD:VD + 1, c % 2, :]).then_inc(o_st[c % 2], 16)

            for b in range(2):
                sp.sem_inc(o_st[b], 32)
            sp.sem_inc(m_in, 16)
            load(0)

            def after_split(h):
                sp.wait_ge(split_a, PIECES * h + PIECES)
                sp.wait_ge(split_p, PIECES * h + PIECES)

            after_split(0)
            load(1)
            maxima(0, 0)

            def head(h, s, more, more2):
                if more:
                    store(h, 0)
                    store(h, 1)
                    if more2:
                        after_split(h + 1)
                        load(h + 2)
                    store(h, 2)
                    maxima(h + 1, 1 - s)
                    store(h, 3)
                else:
                    for c in range(NC_):
                        store(h, c)

            with sp.Fori(0, H // 2 - 1) as t:
                for s in range(2):
                    head(2 * t + s, s, True, True)
            head(H - 2, 0, True, False)
            head(H - 1, 1, False, False)
            for b in range(2):
                sp.wait_ge(o_st[b], 32 * (2 * H + 1))

        @block.tensor
        def _(pe):
            def scores(h, s, u, wait_max):
                c, j = cols[u]
                off = max(0, j - 4 * c) * P
                q = slice(c * CH + off, (c + 1) * CH)
                k = slice(j * P, (j + 1) * P)
                out = psS[u % RING][:, off:CH]
                if wait_max:
                    pe.wait_ge(m_in, 32 * h + 48)
                pe.wait_ge(hi, NU * h + u + 1)
                nc.tensor.matmul(out, kh[:, s, k], qh[:, s, q], start=True, stop=False)
                nc.tensor.matmul(out, kh[0:QKD, s, k], ql[:, s, q], start=False, stop=False)
                diag = j >= 4 * c
                mm = nc.tensor.matmul(out, kl[:, s, k], qh[0:QKD, s, q], start=False, stop=not diag)
                if diag:
                    mm = nc.tensor.matmul(psS[u % RING][:, off:off + P], idb[:], negT[:], start=False, stop=True)
                mm.then_inc(st, 1)

            def products(h, s, u):
                c, j = cols[u]
                off = max(0, j - 4 * c) * P
                pe.wait_ge(lo[u % 2], NU // 2 * h + u // 2 + 1 + RING // 2)
                if j == 0:
                    pe.wait_ge(o_out, 4 * h + c + 1)
                out = psO[c % 2][0:VA, off:CH]
                last = j == 4 * c + 3
                r = u % RING
                nc.tensor.matmul(out, vh[:, s, j, :], ph[:, r, off:CH], start=(j == 0), stop=False)
                nc.tensor.matmul(out, vh[:, s, j, :], pl[:, r, off:CH], start=False, stop=False)
                nc.tensor.matmul(out, vl[:, s, j, :], ph[:, r, off:CH], start=False, stop=last).then_inc(pv, 1)

            def maxima(h, s, v):
                b = (s * NA + v) % 2
                pe.wait_ge(a_max, NA * h + v + 1)
                if v == NA - 1:
                    pe.wait_ge(mmin, h + 1)
                    nc.tensor.transpose(psA[b][0:NT, 0:P], mm_[:], ident).then_inc(a_mm, 1)
                    return
                i, c = rows[v]
                if v == 0:
                    pe.wait_ge(split_a, PIECES * h + PIECES)
                    pe.wait_ge(split_p, PIECES * h + PIECES)
                w = min(CH, (i + 1) * P - c * CH)
                diag = c == i // 4
                mm = nc.tensor.matmul(psA[b][:, 0:w], qh[0:QKD, s, i * P:(i + 1) * P], kh[0:QKD, s, c * CH:c * CH + w], start=True, stop=not diag)
                if diag:
                    mm = nc.tensor.matmul(psA[b][:, w - P:w], idb[:], neg[:], start=False, stop=True)
                mm.then_inc(a_mm, 1)

            pe.sem_inc(pv, RING)
            pe.wait_ge(set_, 9)
            for v in range(NA):
                maxima(0, 0, v)
            for u in range(AHEAD):
                scores(0, 0, u, u == 0)

            def head(h, s, more):
                for u in range(NU):
                    if u + AHEAD < NU:
                        scores(h, s, u + AHEAD, False)
                    elif more:
                        scores(h + 1, 1 - s, u + AHEAD - NU, u + AHEAD == NU)
                    if more:
                        for v in a_at.get(u, []):
                            maxima(h + 1, 1 - s, v)
                    products(h, s, u)

            heads(pe, head)

        @block.scalar
        def _(act):
            def split(h, s, n):
                if n == 0:
                    act.wait_ge(raw_in, 80 * h + 80)
                if n == PIECES - 1:
                    nc.scalar.copy(vh[:, s, :, 0:VD], vraw[:]).then_inc(split_a, 1)
                    return
                t = slice(n % NC_ * CH, (n % NC_ + 1) * CH)
                d, r = ((qh, qraw), (kh, kraw))[n // NC_]
                nc.scalar.copy(d[0:QKD, s, t], r[:, t]).then_inc(split_a, 1)

            act.sem_inc(hi, RING)
            act.sem_inc(o_out, 2)
            for n in range(PIECES):
                split(0, 0, n)

            def copy_out(h, c):
                act.wait_ge(pv, NU * h + [4, 12, 24, 40][c] + RING)
                act.wait_ge(o_st[c % 2], 64 * h + 32 * (c // 2) + 32)
                nc.scalar.copy(ost[:, c % 2, :], psO[c % 2][0:VA, :]).then_inc(o_out, 1)

            def head(h, s, more):
                for u in range(NU):
                    c, j = cols[u]
                    off = max(0, j - 4 * c) * P
                    act.wait_ge(st, NU * h + u + 1)
                    act.wait_ge(lo[u % 2], NU // 2 * h + u // 2 + 1)
                    nc.scalar.activation(pf[:, u % RING, off:CH], psS[u % RING][:, off:CH], ACT.Exp)
                    act.wait_ge(pv, NU * h + u + 1)
                    nc.scalar.activation(ph[:, u % RING, off:CH], psS[u % RING][:, off:CH], ACT.Exp).then_inc(hi, 1)
                    if u in (6, 14, 26):
                        copy_out(h, (6, 14, 26).index(u))
                    if more and u < PIECES:
                        if u == 0:
                            act.wait_ge(pv, NU * h + RING)
                        split(h + 1, 1 - s, u)
                copy_out(h, 3)

            heads(act, head)

        @block.vector
        def _(dve):
            V = nc.vector
            V.tensor_copy(idb[:], cst[:, C_ID:C_ID + P]).then_inc(set_, 1)
            V.tensor_copy(neg[:], cst[:, C_NEG:C_NEG + P]).then_inc(set_, 1)
            V.tensor_copy(negT[:], cst[:, C_NEGT:C_NEGT + P]).then_inc(set_, 1)
            V.tensor_scalar(kh[QKD:KA, :, :], cst[QKD:KA, C_ONE:C_ONE + 1].unsqueeze(2).broadcast_to([2, 2, T]), 1.0, None, ALU.mult).then_inc(set_, 1)
            V.memset(nm[:], -NEG).then_inc(set_, 1)
            dve.sem_inc(lo[1], RING // 2)
            dve.sem_inc(a_max, 2)

            def top(h, s, v):
                b = (s * NA + v) % 2
                if v < NA - 1:
                    i, c = rows[v]
                    w = min(CH, (i + 1) * P - c * CH)
                    dve.wait_ge(a_mm, NA * h + v + 1)
                    V.tensor_reduce(nm[:, i, c:c + 1], psA[b][:, 0:w], AX, ALU.max, negate=True).then_inc(a_max, 1)
                    return
                dve.wait_ge(a_max, NA * h + v + 2)
                V.tensor_reduce(mm_[:].unsqueeze(2), nm[:], AX, ALU.min).then_inc(mmin, 1)
                dve.wait_ge(a_mm, NA * h + v + 1)
                dve.wait_ge(m_in, 32 * h + 16)
                V.tensor_copy(mh[:], psA[b][0:NT, 0:P]).then_inc(mhd, 1)
                dve.wait_ge(mhd, h + 1)
                V.tensor_tensor(ml[:], psA[b][0:NT, 0:P], mh[:], ALU.subtract).then_inc(a_max, 1)
                dve.wait_ge(a_max, NA * h + v + 3)
                dve.sem_inc(mld, 1)

            for n in range(1, PIECES, 2):
                dve.wait_ge(split_a, n + 1)
                t = slice(n % NC_ * CH, (n % NC_ + 1) * CH)
                d, x, r = ((ql, qh, qraw), (kl, kh, kraw))[n // NC_]
                V.tensor_tensor(d[:, 0, t], r[:, t], x[0:QKD, 0, t], ALU.subtract).then_inc(split_p, 1)
            for v in range(NA):
                top(0, 0, v)

            def head(h, s, more):
                for u in range(NU):
                    c, j = cols[u]
                    off = max(0, j - 4 * c) * P
                    r = u % RING
                    if u % 2 == 1:
                        dve.wait_ge(hi, NU * h + u + 1 + RING)
                        V.tensor_tensor(pl[:, r, off:CH], pf[:, r, off:CH], ph[:, r, off:CH], ALU.subtract).then_inc(lo[1], 1)
                    if more:
                        for v in a_at.get(u, []):
                            top(h + 1, 1 - s, v)

            heads(dve, head)

        @block.gpsimd
        def _(pool):
            G_ = nc.gpsimd
            pool.sem_inc(lo[0], RING // 2)
            for s in range(2):
                G_.tensor_copy(vh[:, s, :, VD:VD + 2], cst[:, C_ONE:C_ONE + 2].unsqueeze(1).broadcast_to([P, NT, 2])).then_inc(set_, 1)
                G_.tensor_copy(vl[:, s, :, VD:VD + 2], cst[:, C_ONE + 1:C_ONE + 3].unsqueeze(1).broadcast_to([P, NT, 2])).then_inc(set_, 1)

            def split(h, s, n):
                pool.wait_ge(split_a, PIECES * h + n + 1)
                if n < PIECES - 1:
                    t = slice(n % NC_ * CH, (n % NC_ + 1) * CH)
                    d, x, r = ((ql, qh, qraw), (kl, kh, kraw))[n // NC_]
                    G_.tensor_tensor(d[:, s, t], r[:, t], x[0:QKD, s, t], ALU.subtract).then_inc(split_p, 1)
                else:
                    G_.tensor_tensor(vl[:, s, :, 0:VD], vraw[:], vh[:, s, :, 0:VD], ALU.subtract).then_inc(split_p, 1)

            for n in range(0, PIECES, 2):
                split(0, 0, n)

            def head(h, s, more):
                for u in range(NU):
                    c, j = cols[u]
                    off = max(0, j - 4 * c) * P
                    r = u % RING
                    if u % 2 == 0:
                        pool.wait_ge(hi, NU * h + u + 1 + RING)
                        G_.tensor_tensor(pl[:, r, off:CH], pf[:, r, off:CH], ph[:, r, off:CH], ALU.subtract).then_inc(lo[0], 1)
                    if more and 1 <= u < PIECES + 1:
                        split(h + 1, 1 - s, u - 1)

            heads(pool, head)


def mix(nc, o_d, l_d, conv_d, gates_d, x, w_a, w_b, w_out, x2_d):
    CM = 256
    NM, NQ = T // CM, CM // P
    PARTS = 4 + 4 + KD
    with ExitStack() as ctx:
        s_ = Scope(nc, ctx, "mx")
        wbp, wap = (s_.sb(n, [P, 2, 4, D], F32R) for n in ("wb", "wa"))
        wop = s_.sb("wo", [P, 2, KD, D], F32R)
        ar = s_.sb("ar", [P, 4, CM])
        lr = s_.sb("lr", [P, 4, CM])
        cv = s_.sb("cv", [P, 4, CM])
        aT = s_.sb("aT", [P, 2, 4, CM], F32R)
        cT = s_.sb("cT", [P, 2, 4, CM], F32R)
        gt = s_.sb("gt", [P, 4, 2, CM])
        mT = s_.sb("mT", [P, 2, KD, CM], F32R)
        m2 = s_.sb("m2", [P, 2, 2, CM])
        xr = s_.sb("xr", [P, NQ, D])
        xo = s_.sb("xo", [P, NQ, D])
        psAB = [s_.ps(f"psAB{i}", [P, CH]) for i in range(4)]
        psO = [s_.ps(f"psO{i}", [P, CH]) for i in range(2 * NQ)]
        w_in = [s_.sem(f"w_in{i}") for i in range(4)]
        g_in = [s_.sem(f"g_in{i}") for i in range(4)]
        w_hi, w_lo_v, w_lo_p, ar_in, cv_in, x_in, inverted, divided = (s_.sem(n) for n in (
            "w_hi", "w_lo_v", "w_lo_p", "ar_in", "cv_in", "x_in", "inverted", "divided"))
        in_hi, c_lo, a_lo, ab_done, gated, mixed, m_hi, m_lo, o_mm, o_done, stored = (s_.sem(n) for n in (
            "in_hi", "c_lo", "a_lo", "ab_done", "gated", "mixed", "m_hi", "m_lo", "o_mm", "o_done", "stored"))
        g_v = gates_d.rearrange("(a j p) t -> j p a t", a=2, p=P)

        def weight(i):
            d, w, k = (wbp, w_b, i) if i < 4 else (wap, w_a, i - 4) if i < 8 else (wop, w_out, i - 8)
            return (xr, xo)[i // 2 % 2][:, i % 2, :], w[k * P:(k + 1) * P, :], d[:, 0, k, :], d[:, 1, k, :]

        def chunks(eng, run):
            with eng.Fori(0, NM - 1) as c:
                run(c, True)
            run(NM - 1, False)

        block = ctx.enter_context(nc.Block())

        @block.sync
        def _(sp):
            def rows(c):
                t = bass.ts(c, CM)
                sp.dma_start(ar[:], o_d[:, t].rearrange("(f p) t -> p f t", p=P)).then_inc(ar_in, 16)
                for e in range(2):
                    sp.dma_start(lr[e * VD:(e + 1) * VD, :, :], l_d[e:H:2, t].unsqueeze(0).broadcast_to([VD, H // 2, CM])).then_inc(ar_in, 16)

            def conv(c):
                sp.dma_start(cv[:], conv_d[:, bass.ts(c, CM)].rearrange("(k p) t -> p k t", p=P)).then_inc(cv_in, 16)

            def gates(c, j):
                sp.dma_start(gt[:, j % 4, :, :], g_v[j, :, :, bass.ts(c, CM)]).then_inc(g_in[j % 4], 16)

            def xrows(c):
                sp.dma_start(xr[:], x[bass.ts(c, CM), :].rearrange("(q p) f -> p q f", p=P)).then_inc(x_in, 16)

            sp.sem_inc(stored, 16)
            for i in range(PARTS):
                if i >= 12:
                    sp.wait_ge(w_lo_p, i - 11)
                elif i >= 4:
                    sp.wait_ge(w_lo_v, i - 3)
                stage, src, _hi, _lo = weight(i)
                sp.dma_start(stage, src).then_inc(w_in[i % 4], 16)
                if i == 3:
                    conv(0)
                    rows(0)
                if i == 7:
                    for j in range(4):
                        gates(0, j)
            sp.wait_ge(w_lo_p, PARTS - 8)
            xrows(0)

            def chunk(c, more):
                here = sp.snap(c + 0) if more else c
                after = sp.snap(c + 1) if more else None
                for j in range(4):
                    sp.wait_ge(gated, 16 * c + 2 * j + 6)
                    gates(here, j + 4)
                if more:
                    sp.wait_ge(c_lo, c + 1)
                    conv(after)
                    sp.wait_ge(a_lo, c + 1)
                    rows(after)
                    for j in range(4):
                        sp.wait_ge(gated, 16 * c + 2 * j + 14)
                        gates(after, j)
                sp.wait_ge(o_done, 2 * NQ * c + 4 * NQ)
                sp.dma_start(x2_d[bass.ts(here, CM), :].rearrange("(q p) f -> p q f", p=P), xo[:]).then_inc(stored, 16)
                if more:
                    xrows(after)

            chunks(sp, chunk)
            sp.wait_ge(stored, 16 * NM + 16)

        @block.tensor
        def _(pe):
            pe.sem_inc(o_mm, 2 * NQ)

            def branches(c, first=False):
                for j in range(KD):
                    for a in range(2):
                        n = 2 * j + a
                        if first and j == 0:
                            pe.wait_ge(w_lo_v, 4 * a + 4)
                        if j == 0:
                            pe.wait_ge((c_lo, a_lo)[a], c + 1)
                        pe.wait_ge(gated, 16 * c + n + 1)
                        w, r = ((wbp, cT), (wap, aT))[a]
                        for i, (x_, y_) in enumerate(((0, 0), (1, 0), (0, 1))):
                            for k in range(4):
                                mm = nc.tensor.matmul(psAB[n % 4][:, 0:CM], w[:, x_, k, j * P:(j + 1) * P], r[:, y_, k, :],
                                                      start=(i == 0 and k == 0), stop=(i == 2 and k == 3))
                        mm.then_inc(ab_done, 1)

            def output(c, first):
                if first:
                    pe.wait_ge(w_lo_p, PARTS - 8)
                for n in range(2 * NQ):
                    q, hf = n // 2, n % 2
                    pe.wait_ge(o_done, 2 * NQ * c + n + 1)
                    for k in range(KD):
                        if n == 0:
                            pe.wait_ge(m_lo, KD * c + k + 3)
                        for i, (x_, y_) in enumerate(((0, 0), (1, 0), (0, 1))):
                            mm = nc.tensor.matmul(psO[n][:], mT[:, x_, k, q * P:(q + 1) * P], wop[:, y_, k, hf * CH:(hf + 1) * CH],
                                                  start=(k == 0 and i == 0), stop=(k == KD - 1 and i == 2))
                    mm.then_inc(o_mm, 1)

            branches(0, True)
            output(0, True)
            with pe.Fori(1, NM) as c:
                branches(c)
                output(c, False)

        @block.scalar
        def _(act):
            def high(i):
                act.wait_ge(w_in[i % 4], 16 * (i // 4) + 16)
                stage, _src, hi, _lo = weight(i)
                nc.scalar.copy(hi, stage).then_inc(w_hi, 1)

            def conv_high(c):
                act.wait_ge(cv_in, 16 * c + 16)
                nc.scalar.copy(cT[:, 0], cv[:]).then_inc(in_hi, 1)

            def attention_high(c):
                act.wait_ge(divided, c + 1)
                nc.scalar.copy(aT[:, 0], ar[:]).then_inc(in_hi, 1)

            for i in range(4):
                high(i)
            conv_high(0)
            for i in range(4, 8):
                high(i)
            attention_high(0)
            for i in range(8, PARTS):
                high(i)

            def chunk(c, more):
                for j in range(KD):
                    act.wait_ge(mixed, KD * c + j + 1)
                    if j == 0:
                        act.wait_ge(o_mm, 2 * NQ * c + 2 * NQ)
                    nc.scalar.copy(mT[:, 0, j, :], m2[:, j % 2, 0, :]).then_inc(m_hi, 1)
                if more:
                    act.wait_ge(ab_done, 16 * c + 16)
                    conv_high(c + 1)
                    attention_high(c + 1)

            chunks(act, chunk)

        @block.gpsimd
        def _(pool):
            G_ = nc.gpsimd

            def inputs(c):
                pool.wait_ge(in_hi, 2 * c + 1)
                G_.tensor_tensor(cT[:, 1], cv[:], cT[:, 0], ALU.subtract).then_inc(c_lo, 1)
                pool.wait_ge(in_hi, 2 * c + 2)
                G_.tensor_tensor(aT[:, 1], ar[:], aT[:, 0], ALU.subtract).then_inc(a_lo, 1)

            pool.sem_inc(m_lo, 2)
            inputs(0)
            for i in range(8, PARTS):
                pool.wait_ge(w_hi, i + 1)
                stage, _src, hi, lo = weight(i)
                G_.tensor_tensor(lo, stage, hi, ALU.subtract).then_inc(w_lo_p, 1)

            def chunk(c, more):
                for j in range(KD):
                    pool.wait_ge(m_hi, KD * c + j + 1)
                    G_.tensor_tensor(mT[:, 1, j, :], m2[:, j % 2, 0, :], mT[:, 0, j, :], ALU.subtract).then_inc(m_lo, 1)
                if more:
                    inputs(c + 1)

            chunks(pool, chunk)

        @block.vector
        def _(dve):
            V = nc.vector
            dve.sem_inc(gated, 4)
            dve.sem_inc(o_done, 2 * NQ)

            def divide(c):
                dve.wait_ge(ar_in, 48 * c + 48)
                V.reciprocal(lr[:], lr[:]).then_inc(inverted, 1)
                dve.wait_ge(inverted, c + 1)
                V.tensor_tensor(ar[:], ar[:], lr[:], ALU.mult).then_inc(divided, 1)

            for i in range(8):
                dve.wait_ge(w_hi, i + 1)
                stage, _src, hi, lo = weight(i)
                V.tensor_tensor(lo, stage, hi, ALU.subtract).then_inc(w_lo_v, 1)
                if i == 3:
                    divide(0)

            def chunk(c, more):
                for j in range(KD):
                    dve.wait_ge(g_in[j % 4], 32 * c + 16 * (j // 4) + 16)
                    dve.wait_ge(m_lo, KD * c + j + 1)
                    for a in range(2):
                        n = 2 * j + a
                        dve.wait_ge(ab_done, 16 * c + n + 1)
                        V.tensor_tensor(m2[:, j % 2, a, :], psAB[n % 4][:, 0:CM], gt[:, j % 4, 1 - a, :], ALU.mult).then_inc(gated, 1)
                    dve.wait_ge(gated, 16 * c + 2 * j + 6)
                    V.tensor_tensor(m2[:, j % 2, 0, :], m2[:, j % 2, 0, :], m2[:, j % 2, 1, :], ALU.add).then_inc(mixed, 1)
                if more:
                    divide(c + 1)
                dve.wait_ge(x_in, 16 * c + 16)
                dve.wait_ge(stored, 16 * c + 16)
                for n in range(2 * NQ):
                    q, hf = n // 2, slice(n % 2 * CH, n % 2 * CH + CH)
                    dve.wait_ge(o_mm, 2 * NQ * c + n + 1 + 2 * NQ)
                    V.tensor_tensor(xo[:, q, hf], psO[n][:], xr[:, q, hf], ALU.add).then_inc(o_done, 1)

            chunks(dve, chunk)


def mem_keys_values(nc, memT, w, w_in, kmT, vm):
    with ExitStack() as ctx:
        s_ = Scope(nc, ctx, "mk")
        ps = [s_.ps(f"ps{i}", [P, CH]) for i in range(6)]
        mm_done, taken = s_.sem("mm"), s_.sem("taken")
        block = ctx.enter_context(nc.Block())

        @block.tensor
        def _(pe):
            pe.wait_ge(w_in, 16)
            for h in range(XH):
                for k in range(KD):
                    mm = nc.tensor.matmul(ps[h][:, 0:MEM], w[:, k, h * XD:(h + 1) * XD], memT[:, k, :], start=(k == 0), stop=(k == KD - 1))
                mm.then_inc(mm_done, 1)
            for b in range(MEM // P):
                for k in range(KD):
                    mm = nc.tensor.matmul(ps[4 + b][:], memT[:, k, b * P:(b + 1) * P], w[:, k, XH * XD:], start=(k == 0), stop=(k == KD - 1))
                mm.then_inc(mm_done, 1)

        @block.vector
        def _(dve):
            for n in range(6):
                dve.wait_ge(mm_done, n + 1)
                if n < 4:
                    nc.vector.tensor_copy(kmT[:, n, :], ps[n][:, 0:MEM]).then_inc(taken, 1)
                else:
                    nc.vector.tensor_copy(vm[:, n - 4, :], ps[n][:]).then_inc(taken, 1)


def cross_attention(nc, cst, hT, kmT, vm, wq, wo, w_in, x2_d, x3_d, y_d):
    XS = 1.0 / math.sqrt(XD)
    with ExitStack() as ctx:
        s_ = Scope(nc, ctx, "xa")
        qT = s_.sb("qT", [P, 2, XH, CH])
        pr = s_.sb("pr", [P, 2, 2, MEM])
        pT = s_.sb("pT", [P, XH, 2, CH])
        oT = s_.sb("oT", [P, XH, CH])
        xr = s_.sb("xr", [P, 4, D])
        xo = s_.sb("xo", [P, 4, D])
        nm = s_.sb("nm", [P, 8, 2])
        zero = s_.sb("zero", [P, D])
        zero_set, zeroed = s_.sem("zero_set"), s_.sem("zeroed")
        ls = s_.sb("ls", [P, 8, 2])
        psQ = [s_.ps(f"psQ{i}", [P, CH]) for i in range(2)]
        psS = [s_.ps(f"psS{i}", [P, 2, MEM]) for i in range(2)]
        psT = [s_.ps(f"psT{i}", [P, 2, 2, P]) for i in range(2)]
        psO = [s_.ps(f"psO{i}", [P, CH]) for i in range(2)]
        x_in, q_mm, q_out, scored, maxed, exped = (s_.sem(n) for n in ("x_in", "q_mm", "q_out", "scored", "maxed", "exped"))
        rcp, normed, turned, flat, o_mm, o_out, y_mm, y_out, stored = (s_.sem(n) for n in ("rcp", "normed", "turned", "flat", "o_mm", "o_out", "y_mm", "y_out", "stored"))
        ident = cst[:, C_ID:C_ID + P]
        block = ctx.enter_context(nc.Block())

        @block.sync
        def _(sp):
            sp.wait_ge(zero_set, 1)
            spare = y_d[E * P:, :].rearrange("(p r) d -> r p d", p=P)
            with sp.Fori(0, NB - E) as r:
                sp.dma_start(spare[bass.ds(r, 1)].rearrange("a p d -> p (a d)"), zero[:]).then_inc(zeroed, 16)
            sp.sem_inc(stored, 16)
            with sp.Fori(0, NC_) as c:
                sp.wait_ge(y_out, 8 * c + 8)
                sp.dma_start(xr[:], x2_d[bass.ts(c, CH), :].rearrange("(q p) f -> p q f", p=P)).then_inc(x_in, 16)
                sp.wait_ge(y_out, 8 * c + 16)
                sp.dma_start(x3_d[bass.ts(c, CH), :].rearrange("(q p) f -> p q f", p=P), xo[:]).then_inc(stored, 16)
            sp.wait_ge(stored, 16 * NC_ + 16)
            sp.wait_ge(zeroed, 16 * (NB - E))

        def chunks(eng, run):
            with eng.Fori(0, NC_ // 2 - 1) as t:
                for s in range(2):
                    run(2 * t + s, s, True)
            run(NC_ - 2, 0, True)
            run(NC_ - 1, 1, False)

        @block.tensor
        def _(pe):
            def queries(c, h, ks):
                if ks[0] == 0:
                    pe.wait_ge(q_out, XH * c + h + 1)
                for k in ks:
                    mm = nc.tensor.matmul(psQ[h % 2][:], wq[:, k, h * XD:(h + 1) * XD], hT[:, k, bass.ts(c, CH)], start=(k == 0), stop=(k == KD - 1))
                if ks[-1] == KD - 1:
                    mm.then_inc(q_mm, 1)

            pe.sem_inc(turned, 2)
            pe.wait_ge(w_in, 32)
            for h in range(XH):
                queries(0, h, range(KD))

            def chunk(c, slot, more):
                def score(u):
                    pe.wait_ge(exped, 16 * c + 2 * u + 2)
                    for e in range(2):
                        h = 2 * (u % 2) + e
                        mm = nc.tensor.matmul(psS[u % 2][:, e, :], qT[:, slot, h, u // 2 * P:u // 2 * P + P], kmT[:, h, :], start=True, stop=True)
                    mm.then_inc(scored, 1)

                pe.wait_ge(q_out, XH * c + XH + 2)
                score(0)
                score(1)
                for u in range(8):
                    if more:
                        queries(c + 1, u // 2, range(u % 2 * KD // 2, u % 2 * KD // 2 + KD // 2))
                    pe.wait_ge(normed, 8 * c + u + 1)
                    pe.wait_ge(flat, 8 * c + u + 1)
                    for e in range(2):
                        for b in range(2):
                            mm = nc.tensor.transpose(psT[u % 2][:, e, b, :], pr[:, u % 2, e, b * P:(b + 1) * P], ident)
                    mm.then_inc(turned, 1)
                    if u + 2 < 8:
                        score(u + 2)
                pe.wait_ge(flat, 8 * c + 10)
                for h in range(XH):
                    if h >= 2:
                        pe.wait_ge(o_out, XH * c + h - 1)
                    else:
                        pe.wait_ge(y_out, 8 * c + h + 7)
                    for b in range(2):
                        mm = nc.tensor.matmul(psO[h % 2][:], vm[:, b, h * XD:(h + 1) * XD], pT[:, h, b, :], start=(b == 0), stop=(b == 1))
                    mm.then_inc(o_mm, 1)
                pe.wait_ge(o_out, XH * c + XH)
                for n in range(8):
                    q, hf = n // 2, n % 2
                    if n >= 2:
                        pe.wait_ge(y_out, 8 * c + n + 7)
                    for k in range(XH):
                        mm = nc.tensor.matmul(psO[n % 2][:], oT[:, k, q * P:(q + 1) * P], wo[:, k, hf * CH:(hf + 1) * CH], start=(k == 0), stop=(k == XH - 1))
                    mm.then_inc(y_mm, 1)

            chunks(pe, chunk)

        @block.scalar
        def _(act):
            def take_q(c, slot, h):
                act.wait_ge(q_mm, XH * c + h + 1)
                nc.scalar.mul(qT[:, slot, h, :], psQ[h % 2][:], XS).then_inc(q_out, 1)

            act.sem_inc(q_out, 2)
            act.sem_inc(exped, 4)
            for h in range(XH):
                take_q(0, 0, h)

            def chunk(c, slot, more):
                for u in range(8):
                    act.wait_ge(maxed, 8 * c + u + 1)
                    act.wait_ge(turned, 8 * c + u + 1)
                    for e in range(2):
                        nc.scalar.activation(pr[:, u % 2, e, :], psS[u % 2][:, e, :], ACT.Exp, bias=nm[:, u, e:e + 1],
                                             accum_out=ls[:, u, e:e + 1]).then_inc(exped, 1)
                    if more and u % 2 == 0 and u > 0:
                        take_q(c + 1, 1 - slot, u // 2 - 1)
                if more:
                    take_q(c + 1, 1 - slot, XH - 1)
                for h in range(XH):
                    act.wait_ge(o_mm, XH * c + h + 1)
                    nc.scalar.copy(oT[:, h, :], psO[h % 2][:]).then_inc(o_out, 1)

            chunks(act, chunk)

        @block.vector
        def _(dve):
            V = nc.vector
            V.memset(zero[:], 0.0).then_inc(zero_set, 1)
            dve.sem_inc(flat, 2)
            dve.sem_inc(y_out, 8)

            def chunk(c, slot, more):
                def top(u):
                    dve.wait_ge(scored, 8 * c + u + 1)
                    V.tensor_reduce(nm[:, u, :], psS[u % 2][:], AX, ALU.max, negate=True).then_inc(maxed, 1)

                def norm(u):
                    dve.wait_ge(exped, 16 * c + 2 * u + 6)
                    V.reciprocal(ls[:, u, :], ls[:, u, :]).then_inc(rcp, 1)
                    dve.wait_ge(rcp, 8 * c + u + 1)
                    V.tensor_tensor(pr[:, u % 2, :, :], pr[:, u % 2, :, :], ls[:, u, :].unsqueeze(2).broadcast_to([P, 2, MEM]), ALU.mult).then_inc(normed, 1)

                def flatten(u):
                    dve.wait_ge(turned, 8 * c + u + 3)
                    h = 2 * (u % 2)
                    V.tensor_copy(pT[:, h:h + 2, :, u // 2 * P:u // 2 * P + P], psT[u % 2][:]).then_inc(flat, 1)

                top(0)
                for u in range(8):
                    if u + 1 < 8:
                        top(u + 1)
                    norm(u)
                    if u >= 1:
                        flatten(u - 1)
                flatten(7)
                dve.wait_ge(x_in, 16 * c + 16)
                dve.wait_ge(stored, 16 * c + 16)
                for n in range(8):
                    q, hf = n // 2, slice(n % 2 * CH, n % 2 * CH + CH)
                    dve.wait_ge(y_mm, 8 * c + n + 1)
                    V.tensor_tensor(xo[:, q, hf], psO[n % 2][:], xr[:, q, hf], ALU.add).then_inc(y_out, 1)

            chunks(dve, chunk)


def route(nc, cst, hT, w_r, b_r, tab_d, wts, dest, tab, meta, load_first_experts):
    NR = G + E
    with ExitStack() as ctx:
        s_ = Scope(nc, ctx, "rt")
        wr = s_.sb("wr", [P, KD, NR])
        br = s_.sb("br", [P, NR])
        lT = s_.sb("lT", [NR, T])
        lg = s_.sb("lg", [P, NT, NR])
        gm = s_.sb("gm", [P, NT, 8])
        pg = s_.sb("pg", [P, NT, G])
        eq = s_.sb("eq", [P, NT, 8])
        ci = s_.sb("ci", [P, NT, 1])
        ohg = s_.sb("ohg", [P, NT, 8])
        oh = s_.sb("oh", [P, 2, NT, 8])
        ing = s_.sb("ing", [P, NT, 8])
        big = s_.sb("big", [P, NT, E])
        asg = s_.sb("asg", [P, 2, NT, E])
        mb = s_.sb("mb", [P, NT, E], BF16)
        cp = s_.sb("cp", [P, NT + 1, E], BF16)
        ones = s_.sb("ones", [P, P], BF16)
        ltb = s_.sb("ltb", [P, P], BF16)
        D_ = s_.sb("D_", [P, NT, E])
        cnt = s_.sb("cnt", [P, 8, E])
        cnti = s_.sb("cnti", [P, E], I32)
        df = s_.sb("df", [P, 2, NT])
        d2 = s_.sb("d2", [P, 2, NT], I32)
        df2 = s_.sb("df2", [P, 2, NT])
        tp = s_.sb("tp", [P, 2, NT], I32)
        tok = s_.sb("tok", [P, NT], I32)
        cmp = s_.sb("cmp", [1, 32, E])
        mf = s_.sb("mf", [1, 40])
        zt = s_.sb("zt", [P, 96], I32)
        psL = [s_.ps(f"psL{i}", [P, CH]) for i in range(4)]
        psR = [s_.ps(f"psR{i}", [P, CH]) for i in range(3)]
        psK = s_.ps("psK", [P, CH])
        w_in, mm_l, lt_out, mm_r, step_, ex, mm_k, zero_in, ready, back, zeroed, mset = (s_.sem(n) for n in (
            "w_in", "mm_l", "lt_out", "mm_r", "step", "ex", "mm_k", "zero_in", "ready", "back", "zeroed", "mset"))
        scat = s_.kept("scat")
        group_ready, pair_ready, tok_set = s_.sem("group_ready"), s_.sem("pair_ready"), s_.sem("tok_set")
        block = ctx.enter_context(nc.Block())
        tab_rows = tab_d.rearrange("(p b) o -> p (b o)", p=P)

        @block.sync
        def _(sp):
            sp.dma_start(wr[:], w_r.rearrange("(k p) n -> p k n", p=P)).then_inc(w_in, 16)
            sp.dma_start(br[:], b_r.broadcast_to([P, NR])).then_inc(w_in, 16)
            load_first_experts(sp)
            sp.wait_ge(zeroed, 1)
            sp.dma_start(tab_rows, zt[:]).then_inc(zero_in, 16)
            sp.wait_ge(scat, 16 * 2 * NT)
            sp.dma_start(tab[:], tab_rows).then_inc(back, 16)
            sp.wait_ge(back, 16)

        @block.tensor
        def _(pe):
            pe.wait_ge(w_in, 32)
            for c in range(4):
                for k in range(KD):
                    mm = nc.tensor.matmul(psL[c][0:NR, :], wr[:, k, :], hT[:, k, c * CH:(c + 1) * CH], start=(k == 0), stop=(k == KD - 1))
                mm.then_inc(mm_l, 1)
            for i in range(NT):
                if i % 4 == 0:
                    pe.wait_ge(lt_out, i // 4 + 1)
                mm = nc.tensor.transpose(psR[i // 6][:, i % 6 * NR:i % 6 * NR + NR], lT[:, i * P:(i + 1) * P], cst[0:NR, C_ID:C_ID + NR])
            mm.then_inc(mm_r, 1)
            pe.wait_ge(ready, 1)
            for q in range(2):
                nc.tensor.matmul(psL[q][:], ltb[:], mb[:, 8 * q:8 * q + 8, :], start=True, stop=False)
                nc.tensor.matmul(psL[q][:], ones[:], cp[:, 8 * q:8 * q + 8, :], start=False, stop=True)
            nc.tensor.matmul(psK[:, 0:E], ones[:], cp[:, NT, :], start=True, stop=True).then_inc(mm_k, 1)

        @block.scalar
        def _(act):
            act.wait_ge(group_ready, 1)
            nc.scalar.activation(pg[:], pg[:], ACT.Exp).then_inc(ex, 1)
            act.wait_ge(pair_ready, 1)
            nc.scalar.activation(gm[:, :, 2:3], gm[:, :, 2:3], ACT.Exp).then_inc(ex, 1)

        @block.vector
        def _(dve):
            V = nc.vector
            n = [0]

            def link(ins):
                n[0] += 1
                ins.then_inc(step_, 1)
                dve.wait_ge(step_, n[0])

            def bc(x, shape):
                return x.broadcast_to(shape)

            link(V.memset(zt[:], 1 << 20))
            dve.sem_inc(zeroed, 1)
            link(V.memset(ones[:], 1.0))
            link(V.tensor_copy(ltb[:], cst[:, C_LT:C_LT + P]))
            for c in range(4):
                dve.wait_ge(mm_l, c + 1)
                V.tensor_copy(lT[:, c * CH:(c + 1) * CH], psL[c][0:NR, :]).then_inc(lt_out, 1)
            dve.wait_ge(mm_r, 1)
            dve.wait_ge(w_in, 32)
            for r in range(3):
                m = min(6, NT - 6 * r)
                link(V.tensor_tensor(lg[:, 6 * r:6 * r + m, :], psR[r][:, 0:m * NR].rearrange("p (a b) -> p a b", b=NR),
                                     br[:].unsqueeze(1).broadcast_to([P, m, NR]), ALU.add))
            S8 = [P, NT, 8]
            iota8 = cst[:, C_IOTA:C_IOTA + 8].unsqueeze(1).broadcast_to(S8)

            def pick(vals, mx, out):
                link(V.tensor_tensor(eq[:], vals, bc(mx, S8), ALU.is_equal))
                link(V.scalar_tensor_tensor(eq[:], eq[:], -64.0, iota8, ALU.mult, ALU.add))
                link(V.tensor_reduce(ci[:], eq[:], AX, ALU.min))
                link(V.tensor_scalar(ci[:], ci[:], 64.0, None, ALU.add))
                link(V.tensor_tensor(out, iota8, bc(ci[:], S8), ALU.is_equal))

            gl = lg[:, :, 0:G]
            link(V.tensor_reduce(gm[:, :, 0:1], gl, AX, ALU.max))
            link(V.tensor_tensor(pg[:], gl, bc(gm[:, :, 0:1], S8), ALU.subtract))
            dve.sem_inc(group_ready, 1)
            pick(gl, gm[:, :, 0:1], ohg[:])
            el = lg[:, :, G:].rearrange("p t (g e) -> p t g e", g=G)
            b4 = big[:].rearrange("p t (g e) -> p t g e", g=G)
            S4 = [P, NT, G, EG]
            link(V.tensor_tensor(b4, el, ohg[:].unsqueeze(3).broadcast_to(S4), ALU.mult))
            link(V.tensor_reduce(ing[:], big[:].rearrange("p t (g e) -> p t e g", g=G), AX, ALU.add))
            link(V.tensor_reduce(gm[:, :, 1:2], ing[:], AX, ALU.max))
            pick(ing[:], gm[:, :, 1:2], oh[:, 0])
            link(V.scalar_tensor_tensor(ing[:], oh[:, 0], NEG, ing[:], ALU.mult, ALU.add))
            link(V.tensor_reduce(gm[:, :, 2:3], ing[:], AX, ALU.max))
            pick(ing[:], gm[:, :, 2:3], oh[:, 1])
            link(V.tensor_tensor(gm[:, :, 2:3], gm[:, :, 2:3], gm[:, :, 1:2], ALU.subtract))
            dve.sem_inc(pair_ready, 1)
            for a in range(2):
                link(V.tensor_tensor(asg[:, a].rearrange("p t (g e) -> p t g e", g=G), ohg[:].unsqueeze(3).broadcast_to(S4),
                                     oh[:, a].unsqueeze(2).broadcast_to(S4), ALU.mult))
            link(V.tensor_tensor(mb[:], asg[:, 0], asg[:, 1], ALU.add))
            link(V.memset(cp[:, 0, :], 0.0))
            for i in range(NT):
                link(V.tensor_tensor(cp[:, i + 1, :], cp[:, i, :], mb[:, i, :], ALU.add))
            dve.sem_inc(ready, 1)
            dve.wait_ge(ex, 2)
            link(V.tensor_reduce(gm[:, :, 3:4], pg[:], AX, ALU.add))
            link(V.tensor_scalar(gm[:, :, 4:5], gm[:, :, 2:3], 1.0, None, ALU.add))
            link(V.tensor_tensor(gm[:, :, 3:4], gm[:, :, 3:4], gm[:, :, 4:5], ALU.mult))
            link(V.reciprocal(wts[:, :, 0:1], gm[:, :, 3:4]))
            link(V.tensor_tensor(wts[:, :, 1:2], wts[:, :, 0:1], gm[:, :, 2:3], ALU.mult))
            dve.wait_ge(mm_k, 1)
            link(V.tensor_scalar(cnti[:], psK[:, 0:E], 127.0, None, ALU.add))
            link(V.tensor_scalar(cnti[:], cnti[:], 7, None, ALU.arith_shift_right))
            link(V.tensor_copy(cnt[:, 0, :], cnti[:]))
            link(V.tensor_scalar(cnt[:, 0, :], cnt[:, 0, :], 1.0, 0.0, ALU.subtract, ALU.max))
            link(V.tensor_copy(cnt[:, 1, :], cnt[:, 0, :]))
            for d in range(6):
                a, b, w = 1 + d % 2, 2 - d % 2, 1 << d
                link(V.tensor_copy(cnt[:, b, 0:w], cnt[:, a, 0:w]))
                link(V.tensor_tensor(cnt[:, b, w:], cnt[:, a, w:], cnt[:, a, 0:E - w], ALU.add))
            link(V.tensor_tensor(cnt[:, 3, :], cnt[:, 1, :], cnt[:, 0, :], ALU.subtract))
            link(V.tensor_scalar(cnt[:, 3, :], cnt[:, 3, :], float(E - 1), float(P), ALU.add, ALU.mult))
            link(V.tensor_tensor(cnt[:, 3, :], cnt[:, 3, :], cst[:, C_E128:C_E128 + E], ALU.subtract))
            for q in range(2):
                sl = slice(8 * q, 8 * q + 8)
                rk = psL[q][:].rearrange("p (t e) -> p t e", e=E)
                S3 = [P, 8, E]
                link(V.scalar_tensor_tensor(D_[:, sl, :], rk, float(P), cnt[:, 3, :].unsqueeze(1).broadcast_to(S3), ALU.is_ge, ALU.mult))
                link(V.tensor_tensor(D_[:, sl, :], D_[:, sl, :], rk, ALU.add))
            link(V.tensor_tensor(D_[:], D_[:], cst[:, C_E128:C_E128 + E].unsqueeze(1).broadcast_to([P, NT, E]), ALU.add))
            for a in range(2):
                link(V.tensor_tensor(big[:], asg[:, a], D_[:], ALU.mult))
                link(V.tensor_reduce(df[:, a, :].unsqueeze(2), big[:], AX, ALU.add))
            link(V.tensor_copy(dest[:], df[:]))
            link(V.tensor_scalar(d2[:], dest[:], 7, None, ALU.arith_shift_right))
            link(V.tensor_copy(df2[:], d2[:]))
            link(V.scalar_tensor_tensor(df[:], df2[:], -float(P), df[:], ALU.mult, ALU.add))
            link(V.scalar_tensor_tensor(df[:], df[:], 96.0, df2[:], ALU.mult, ALU.add))
            link(V.tensor_copy(tp[:], df[:]))
            io32 = cst[0:1, C_IOTA:C_IOTA + 32].unsqueeze(2).broadcast_to([1, 32, E])
            link(V.tensor_tensor(cmp[:], cnt[0:1, 1, :].unsqueeze(1).broadcast_to([1, 32, E]), io32, ALU.is_le))
            link(V.tensor_reduce(mf[:, 0:32].unsqueeze(2), cmp[:], AX, ALU.add))
            link(V.tensor_scalar(mf[:, 0:32], mf[:, 0:32], float(E - 1), None, ALU.min))
            link(V.tensor_copy(mf[:, 32:33], cnt[0:1, 1, E - 1:E]))
            link(V.tensor_copy(meta[:, 0:33], mf[:, 0:33]))
            dve.sem_inc(mset, 1)

        @block.gpsimd
        def _(pool):
            nc.gpsimd.iota(tok[:], [[P, NT]], base=0, channel_multiplier=1).then_inc(tok_set, 1)
            pool.wait_ge(tok_set, 1)
            pool.wait_ge(mset, 1)
            pool.wait_ge(zero_in, 16)
            for a in range(2):
                for i in range(NT):
                    nc.gpsimd.indirect_dma_start(tab_d, bass.IndirectOffsetOnAxis(ap=tp[:, a, i:i + 1].bitcast(U32), axis=0), tok[:, i:i + 1], None).then_inc(scat, 16)


def experts(nc, cst, h_d, w_gu, w_dn, y_d, tab, meta, wg, wd, g_in, d_in):
    with ExitStack() as ctx:
        s_ = Scope(nc, ctx, "ex")
        ix = s_.sb("ix", [P, 2], I32)
        idle = s_.sb("idle", [1, 8])
        idle_set = s_.sem("idle_set")
        xg = s_.sb("xg", [P, 2, D])
        xT = s_.sb("xT", [P, 2, KD, P])
        sg = s_.sb("sg", [P, 2, FF])
        hm = s_.sb("hm", [P, 2, FF])
        hT = s_.sb("hT", [P, 2, 2, P])
        y = s_.sb("y", [P, 2, D])
        psX = [s_.ps(f"psX{i}", [P, 4, P]) for i in range(2)]
        psG = [s_.ps(f"psG{i}", [P, 2 * FF]) for i in range(2)]
        psH = s_.ps("psH", [P, 2, P])
        psY = [s_.ps(f"psY{i}", [P, CH]) for i in range(2)]
        x_in = [s_.kept("x_in0"), s_.kept("x_in1")]
        st = [s_.sem("st0"), s_.sem("st1")]
        ixd, turned, xa, xv, up, sig, gt, hid, hturn, hcopy, down, ya, yv = (s_.sem(n) for n in (
            "ixd", "turned", "xa", "xv", "up", "sig", "gt", "hid", "hturn", "hcopy", "down", "ya", "yv"))
        ident = cst[:, C_ID:C_ID + P]
        block = ctx.enter_context(nc.Block())

        def overflow(eng, run):
            n_ovf = eng.value_load(meta[0:1, 32:33], min_val=0, max_val=OVF)
            with eng.If(n_ovf > 0):
                with eng.Fori(0, OVF) as o:
                    with eng.If(o < n_ovf):
                        run(o + E)

        @block.sync
        def _(sp):
            def dyn(e, s, n_up, n_down):
                sp.wait_ge(up, n_up)
                sp.dma_start(wg[:, s], w_gu[bass.ds(e, 1)].rearrange("a (k p) n -> p (a k) n", p=P)).then_inc(g_in[s], 16)
                sp.wait_ge(down, n_down)
                sp.dma_start(wd[:, s], w_dn[bass.ds(e, 1)].rearrange("a (k p) n -> p (a k) n", p=P)).then_inc(d_in[s], 16)

            with sp.Fori(0, E // 2 - 1) as t:
                for s in range(2):
                    dyn(2 * t + (s + 2), s, 2 * t + (s + 1), 2 * t + (s + 1))

            def more(b):
                e = sp.value_load(meta[0:1, bass.ds(b - E, 1)], min_val=0, max_val=E - 1)
                dyn(e, 0, b, b)

            overflow(sp, more)

        @block.gpsimd
        def _(pool):
            def gather(b, s, first=False):
                if not first:
                    pool.wait_ge(turned, b - 1)
                nc.gpsimd.tensor_copy(ix[:, s:s + 1], tab[:, bass.ds(b, 1)]).then_inc(ixd, 1)
                pool.wait_ge(ixd, b + 1)
                nc.gpsimd.tensor_tensor(idle[:], idle[:], idle[:], ALU.add)
                nc.gpsimd.indirect_dma_start(xg[:, s, :], None, h_d, bass.IndirectOffsetOnAxis(ap=ix[:, s:s + 1].bitcast(U32), axis=0),
                                             bounds_check=T - 1, oob_is_err=False).then_inc(x_in[s], 16)

            nc.gpsimd.memset(idle[:], 0.0).then_inc(idle_set, 1)
            nc.gpsimd.memset(xg[:], 0.0).then_inc(idle_set, 1)
            pool.wait_ge(idle_set, 2)
            gather(0, 0, True)
            gather(1, 1, True)
            with pool.Fori(1, E // 2) as t:
                for s in range(2):
                    gather(2 * t + s, s)

            def more(b):
                pool.wait_ge(turned, b)
                gather(b, 0)

            overflow(pool, more)

        @block.tensor
        def _(pe):
            def turn(b, s, nx, first=False):
                pe.wait_ge(x_in[s], nx)
                if not first:
                    pe.wait_ge(xa, b)
                    pe.wait_ge(xv, b)
                for k in range(KD):
                    mm = nc.tensor.transpose(psX[k // 4][:, k % 4, :], xg[:, s, k * P:(k + 1) * P], ident)
                mm.then_inc(turned, 1)

            def gate_up(b, s, nw, free=None):
                pe.wait_ge(g_in[s], nw)
                pe.wait_ge(xa, b + 1)
                pe.wait_ge(xv, b + 1)
                if free is not None:
                    pe.wait_ge(hid, free + 1)
                for k in range(KD):
                    mm = nc.tensor.matmul(psG[s][:], xT[:, s, k, :], wg[:, s, k, :], start=(k == 0), stop=(k == KD - 1))
                mm.then_inc(up, 1)

            def turn_hidden(b, s):
                pe.wait_ge(hid, b + 2)
                pe.wait_ge(hcopy, b + 1)
                for k in range(2):
                    mm = nc.tensor.transpose(psH[:, k, :], hm[:, s, k * P:(k + 1) * P], ident)
                mm.then_inc(hturn, 1)

            def go_down(b, s, nw):
                pe.wait_ge(d_in[s], nw)
                pe.wait_ge(hcopy, b + 2)
                pe.wait_ge(ya, b + 1)
                pe.wait_ge(yv, b + 1)
                for f in range(2):
                    for k in range(2):
                        mm = nc.tensor.matmul(psY[f][:], hT[:, s, k, :], wd[:, s, k, f * CH:(f + 1) * CH], start=(k == 0), stop=(k == 1))
                mm.then_inc(down, 1)

            turn(0, 0, 16, True)
            gate_up(0, 0, 16)
            turn(1, 1, 16)
            with pe.Fori(0, E // 2 - 1) as t:
                for s in (1, 0):
                    b = 2 * t + (2 - s)
                    prev = 2 * t + (1 - s)
                    gate_up(b, s, 16 * t + 16 * (2 - s), prev)
                    turn_hidden(prev, 1 - s)
                    turn(2 * t + (3 - s), 1 - s, 16 * t + 32)
                    go_down(prev, 1 - s, 16 * t + 16)
            gate_up(E - 1, 1, 16 * (E // 2), E - 2)
            turn_hidden(E - 2, 0)
            go_down(E - 2, 0, 16 * (E // 2))
            turn_hidden(E - 1, 1)
            go_down(E - 1, 1, 16 * (E // 2))

            def more(b):
                nw = 16 * (b - E) + 16 * (E // 2 + 1)
                turn(b, 0, nw)
                gate_up(b, 0, nw, b)
                turn_hidden(b, 0)
                go_down(b, 0, nw)

            overflow(pe, more)

        @block.scalar
        def _(act):
            def take_x(b, s, first=False):
                act.wait_ge(turned, b + 1)
                if not first:
                    act.wait_ge(up, b - 1)
                nc.scalar.copy(xT[:, s, 0:4, :], psX[0][:]).then_inc(xa, 1)

            def sigmoid(b, s):
                act.wait_ge(up, b + 1)
                nc.scalar.activation(sg[:, s, :], psG[s][:, 0:FF], ACT.Sigmoid).then_inc(sig, 1)

            def take_h(b, s):
                act.wait_ge(hturn, b + 1)
                nc.scalar.copy(hT[:, s], psH[:]).then_inc(hcopy, 1)

            def take_y(b, s, n):
                act.wait_ge(down, b + 1)
                act.wait_ge(st[s], n + 16)
                nc.scalar.copy(y[:, s, 0:CH], psY[0][:]).then_inc(ya, 1)
                act.wait_ge(ya, b + 2)
                act.wait_ge(yv, b + 2)
                act.dma_start(y_d[bass.ts(b, P), :], y[:, s, :]).then_inc(st[s], 16)

            act.sem_inc(hcopy, 1)
            act.sem_inc(ya, 1)
            for s in range(2):
                act.sem_inc(st[s], 16)
            take_x(0, 0, True)
            sigmoid(0, 0)
            take_x(1, 1, True)
            with act.Fori(0, E // 2 - 1) as t:
                for s in (1, 0):
                    prev = 2 * t + (1 - s)
                    sigmoid(2 * t + (2 - s), s)
                    take_h(prev, 1 - s)
                    take_x(2 * t + (3 - s), 1 - s)
                    take_y(prev, 1 - s, 16 * t)
            sigmoid(E - 1, 1)
            take_h(E - 2, 0)
            take_y(E - 2, 0, 16 * (E // 2 - 1))
            take_h(E - 1, 1)
            take_y(E - 1, 1, 16 * (E // 2 - 1))
            act.wait_ge(st[0], 16 * (E // 2) + 16)
            act.wait_ge(st[1], 16 * (E // 2) + 16)

            def more(b):
                take_x(b, 0)
                sigmoid(b, 0)
                take_h(b, 0)
                n = 16 * (b - E) + 16 * (E // 2)
                take_y(b, 0, n)
                act.wait_ge(st[0], n + 32)
                nc.scalar.copy(sg[0:1, 0, 0:8], cst[0:1, 0:8])

            overflow(act, more)

        @block.vector
        def _(dve):
            V = nc.vector

            def take_x(b, s, first=False):
                dve.wait_ge(turned, b + 1)
                if not first:
                    dve.wait_ge(up, b - 1)
                V.tensor_copy(xT[:, s, 4:8, :], psX[1][:]).then_inc(xv, 1)

            def hidden(b, s):
                dve.wait_ge(sig, b + 1)
                V.tensor_tensor(sg[:, s, :], psG[s][:, 0:FF], sg[:, s, :], ALU.mult).then_inc(gt, 1)
                dve.wait_ge(gt, b + 1)
                V.tensor_tensor(hm[:, s, :], psG[s][:, FF:], sg[:, s, :], ALU.mult).then_inc(hid, 1)

            def take_y(b, s, n):
                dve.wait_ge(down, b + 1)
                dve.wait_ge(st[s], n + 16)
                V.tensor_copy(y[:, s, CH:], psY[1][:]).then_inc(yv, 1)

            dve.sem_inc(hid, 1)
            dve.sem_inc(yv, 1)
            take_x(0, 0, True)
            hidden(0, 0)
            take_x(1, 1, True)
            with dve.Fori(0, E // 2 - 1) as t:
                for s in (1, 0):
                    prev = 2 * t + (1 - s)
                    hidden(2 * t + (2 - s), s)
                    take_x(2 * t + (3 - s), 1 - s)
                    take_y(prev, 1 - s, 16 * t)
            hidden(E - 1, 1)
            take_y(E - 2, 0, 16 * (E // 2 - 1))
            take_y(E - 1, 1, 16 * (E // 2 - 1))

            def more(b):
                take_x(b, 0)
                hidden(b, 0)
                take_y(b, 0, 16 * (b - E) + 16 * (E // 2))

            overflow(dve, more)


def combine(nc, x3_d, y_d, wts, dest, g, out):
    R = 4
    with ExitStack() as ctx:
        s_ = Scope(nc, ctx, "cb")
        xr = s_.sb("xr", [P, R, D])
        ys = s_.sb("ys", [P, R, 2, D])
        sq = s_.sb("sq", [P, D])
        yo = s_.sb("yo", [P, 2, D])
        gb = s_.sb("gb", [P, D])
        st = s_.sb("st", [P, 2, 3])
        ix = s_.sb("ix", [P, R, 2], I32)
        idle = s_.sb("idle", [1, 8])
        eps = s_.sb("eps", [P, 1])
        x_in = [s_.sem(f"x_in{i}") for i in range(R)]
        y_in = [s_.kept(f"y_in{i}") for i in range(R)]
        stored = [s_.sem(f"stored{i}") for i in range(2)]
        g_in, eps_set, idle_set, ixd, first_added, added, sq_done, rms_done, rcp_done, done = (s_.sem(n) for n in (
            "g_in", "eps_set", "idle_set", "ixd", "first_added", "added", "sq_done", "rms_done", "rcp_done", "done"))
        block = ctx.enter_context(nc.Block())

        @block.sync
        def _(sp):
            def load(i, s):
                sp.dma_start(xr[:, s, :], x3_d[bass.ts(i, P), :]).then_inc(x_in[s], 16)

            def store(i, s):
                sp.wait_ge(done, i + 1)
                sp.dma_start(out[bass.ts(i, P), :], yo[:, s % 2, :]).then_inc(stored[s % 2], 16)

            for e in range(2):
                sp.sem_inc(stored[e], 16)
            for s in range(R):
                load(s, s)
            sp.dma_start(gb[:], g.broadcast_to([P, D])).then_inc(g_in, 16)
            with sp.Fori(0, NT // R - 1) as t:
                for s in range(R):
                    store(R * t + s, s)
                    load(R * t + (s + R), s)
            for s in range(R):
                store(NT - R + s, s)
            for e in range(2):
                sp.wait_ge(stored[e], 16 * (NT // 2) + 16)

        @block.gpsimd
        def _(pool):
            def gather(i, s, first=False):
                if not first:
                    pool.wait_ge(added, i - (R - 1))
                for a in range(2):
                    nc.gpsimd.tensor_copy(ix[:, s, a:a + 1], dest[:, a, bass.ds(i, 1)]).then_inc(ixd, 1)
                pool.wait_ge(ixd, 2 * i + 2)
                nc.gpsimd.tensor_tensor(idle[:], idle[:], idle[:], ALU.add)
                for a in range(2):
                    nc.gpsimd.indirect_dma_start(ys[:, s, a, :], None, y_d, bass.IndirectOffsetOnAxis(ap=ix[:, s, a:a + 1].bitcast(U32), axis=0)).then_inc(y_in[s], 16)

            nc.gpsimd.memset(idle[:], 0.0).then_inc(idle_set, 1)
            pool.wait_ge(idle_set, 1)
            for s in range(R):
                gather(s, s, True)
            with pool.Fori(1, NT // R) as t:
                for s in range(R):
                    gather(R * t + s, s)

        def tiles(eng, add, norm):
            add(0, 0)
            with eng.Fori(0, NT // R - 1) as t:
                for s in range(R):
                    add(t, s + 1)
                    norm(t, s)
            for s in range(R):
                if s + 1 < R:
                    add(NT // R - 1, s + 1)
                norm(NT // R - 1, s)

        @block.vector
        def _(dve):
            V = nc.vector
            V.memset(eps[:], EPS).then_inc(eps_set, 1)
            dve.wait_ge(g_in, 16)

            def add(t, s):
                i, r, n = R * t + s, s % R, 16 * t + 16 * (s // R + 1)
                dve.wait_ge(x_in[r], n)
                dve.wait_ge(y_in[r], 32 * t + 32 * (s // R + 1))
                V.scalar_tensor_tensor(xr[:, r, :], ys[:, r, 0, :], wts[:, bass.ds(i, 1), 0], xr[:, r, :], ALU.mult, ALU.add).then_inc(first_added, 1)
                dve.wait_ge(first_added, i + 1)
                V.scalar_tensor_tensor(xr[:, r, :], ys[:, r, 1, :], wts[:, bass.ds(i, 1), 1], xr[:, r, :], ALU.mult, ALU.add).then_inc(added, 1)

            def norm(t, s):
                i = R * t + s
                dve.wait_ge(rms_done, i + 1)
                V.reciprocal(st[:, s % 2, 2:3], st[:, s % 2, 1:2]).then_inc(rcp_done, 1)
                dve.wait_ge(rcp_done, i + 1)
                dve.wait_ge(stored[s % 2], 16 * (R // 2) * t + 16 * (s // 2 + 1))
                V.scalar_tensor_tensor(yo[:, s % 2, :], xr[:, s % R, :], st[:, s % 2, 2:3], gb[:], ALU.mult, ALU.mult).then_inc(done, 1)

            tiles(dve, add, norm)

        @block.scalar
        def _(act):
            act.wait_ge(eps_set, 1)
            with act.Fori(0, NT // R) as t:
                for s in range(R):
                    i = R * t + s
                    act.wait_ge(added, i + 1)
                    nc.scalar.activation(sq[:], xr[:, s, :], ACT.Square, accum_out=st[:, s % 2, 0:1]).then_inc(sq_done, 1)
                    act.wait_ge(sq_done, i + 1)
                    nc.scalar.activation(st[:, s % 2, 1:2], st[:, s % 2, 0:1], ACT.Sqrt, bias=eps[:], scale=1.0 / D).then_inc(rms_done, 1)


def program(nc, a, out):
    def scratch(name, shape, dt=F32):
        return nc.dram_tensor(name, shape, dt).ap()

    gates_d = scratch("gates_d", (2 * D, T))
    conv_d = scratch("conv_d", (CW, T))
    qn_d, qr_d = scratch("qn_d", (H * NOPE, T)), scratch("qr_d", (H * ROPE, T))
    kn_d, kr_d = scratch("kn_d", (H * NOPE, T)), scratch("kr_d", (ROPE, T))
    v_d = scratch("v_d", (T, H * VD))
    o_d, l_d = scratch("o_d", (H * VD, T)), scratch("l_d", (H, T))
    x2_d, x3_d, h_d = scratch("x2_d", (T, D)), scratch("x3_d", (T, D)), scratch("h_d", (T, D))
    tab_d = scratch("tab_d", (P * 96, 1), I32)
    y_d = scratch("y_d", (NB * P, D))
    x = a["x"]
    with ExitStack() as outer:
        g_ = Scope(nc, outer, "all")
        cst = g_.sb("cst", [P, C_END])
        vec = g_.sb("vec", [P, V_END])
        c_in = g_.sem("c_in")
        with nc.Block() as block:
            @block.sync
            def _(sp):
                sp.dma_start(cst[:], a["consts"]).then_inc(c_in, 16)
                sp.dma_start(vec[:], a["vecs"]).then_inc(c_in, 16)
                sp.wait_ge(c_in, 32)
        with ExitStack() as front:
            f_ = Scope(nc, front, "fr")
            cqT = f_.sb("cqT", [P, 2, T])
            ckvT = f_.sb("ckvT", [P, T])
            krT = f_.sb("krT", [2 * ROPE, T])
            cosT = f_.sb("cosT", [P, T])
            sinT = f_.sb("sinT", [P, T])
            with ExitStack() as halves:
                p_ = Scope(nc, halves, "hv")
                hh = p_.sb("hh", [P, KD, TH], F32R)
                hl = p_.sb("hl", [P, KD, TH], F32R)
                halo = p_.sb("halo", [P, 2 * CW // P])
                for n_tag, p_tag, t0 in (("n0", "pi", 0), ("n1", "pj", TH)):
                    norm_transpose(nc, n_tag, cst, x[t0:t0 + TH, :], a["g_mix"], hh, TH // P, low=hl)
                    project(nc, p_tag, cst, vec, hh, hl, a["w_slabs"], a["positions"], t0, halo, gates_d, conv_d, cqT, ckvT, krT, cosT, sinT)
            latents(nc, cst, vec, cqT, ckvT, krT, cosT, sinT, a["w_uq"], a["w_uk"], a["w_uv"], qn_d, qr_d, kn_d, kr_d, v_d)
        attention(nc, cst, qn_d, qr_d, kn_d, kr_d, v_d, o_d, l_d)
        mix(nc, o_d, l_d, conv_d, gates_d, x, a["w_branch_a"], a["w_branch_b"], a["w_out"], x2_d)
        clear_semaphores(nc)
        with ExitStack() as mid:
            m_ = Scope(nc, mid, "mi")
            kmT = m_.sb("kmT", [P, XH, MEM])
            vm = m_.sb("vm", [P, MEM // P, XH * XD])
            with nc.sbuf_tensor("memT", [P, KD, MEM], F32) as memT:
                with ExitStack() as mem:
                    k_ = Scope(nc, mem, "mk")
                    w_kv = k_.sb("w", [P, KD, 2 * XH * XD])
                    w_in = k_.sem("w_in")
                    norm_transpose(nc, "nm", cst, a["mem"], a["g_mem"], memT, MEM // P,
                                   ask=lambda sp: sp.dma_start(w_kv[:], a["w_kv_mem"].rearrange("(k p) n -> p k n", p=P)).then_inc(w_in, 16))
                    mem_keys_values(nc, memT, w_kv, w_in, kmT, vm)
            wq = m_.sb("wq", [P, KD, XH * XD])
            wo = m_.sb("wo", [P, XH, D])
            w_in = m_.sem("w_in")

            def ask(sp):
                sp.dma_start(wq[:], a["w_q_mem"].rearrange("(k p) n -> p k n", p=P)).then_inc(w_in, 16)
                sp.dma_start(wo[:], a["w_o_mem"].rearrange("(k p) n -> p k n", p=P)).then_inc(w_in, 16)

            with nc.sbuf_tensor("hT2", [P, KD, T], F32) as hT:
                norm_transpose(nc, "n2", cst, x2_d, a["g_xattn"], hT, NT, ask=ask)
                cross_attention(nc, cst, hT, kmT, vm, wq, wo, w_in, x2_d, x3_d, y_d)
        clear_semaphores(nc)
        with ExitStack() as back:
            b_ = Scope(nc, back, "ba")
            wts = b_.sb("wts", [P, NT, 2])
            dest = b_.sb("dest", [P, 2, NT], I32)
            tab = b_.sb("tab", [P, 96], I32)
            meta = b_.sb("meta", [1, 40], I32)
            wg = b_.sb("wg", [P, 2, KD, 2 * FF])
            wd = b_.sb("wd", [P, 2, 2, D])
            g_in = [b_.sem("g_in0"), b_.sem("g_in1")]
            d_in = [b_.sem("d_in0"), b_.sem("d_in1")]

            def load_first_experts(sp):
                for e in range(2):
                    sp.dma_start(wg[:, e], a["w_gate_up"][e].rearrange("(k p) n -> p k n", p=P)).then_inc(g_in[e], 16)
                    sp.dma_start(wd[:, e], a["w_down"][e].rearrange("(k p) n -> p k n", p=P)).then_inc(d_in[e], 16)

            with nc.sbuf_tensor("hT3", [P, KD, T], F32) as hT:
                norm_transpose(nc, "n3", cst, x3_d, a["g_moe"], hT, NT, h_d)
                route(nc, cst, hT, a["w_r"], a["b_r"], tab_d, wts, dest, tab, meta, load_first_experts)
            experts(nc, cst, h_d, a["w_gate_up"], a["w_down"], y_d, tab, meta, wg, wd, g_in, d_in)
            combine(nc, x3_d, y_d, wts, dest, a["g_final"], out)


def constants():
    c = np.zeros((P, C_END), np.float32)
    p = np.arange(P)
    c[:, C_ID:C_ID + P] = np.eye(P)
    c[:, C_NEG:C_NEG + P] = np.where(p[None, :] > p[:, None], NEG, 0.0)
    c[:, C_LT:C_LT + P] = p[:, None] < p[None, :]
    c[:, C_IOTA:C_IOTA + 64] = np.arange(64)
    c[:, C_INV] = (10000.0 ** (-np.arange(0, ROPE, 2) / ROPE))[p % 16]
    c[:, C_SGN] = np.where(p % 32 < 16, -1.0, 1.0)
    c[:, C_NEGT:C_NEGT + P] = np.where(p[:, None] > p[None, :], NEG, 0.0)
    c[:, C_ONE] = 1.0
    c[:, C_E128:C_E128 + E] = P * np.arange(E)
    return c


def kernel(**inputs):
    import concourse.bacc as bacc
    from concourse.bass_utils import run_bass_kernel_spmd

    w = {n: np.asarray(v) for n, v in inputs.items()}
    w_in = w["w_in"][0]
    LQ, LKV = w["g_cq"].shape[1], w["g_ckv"].shape[1]
    kr = w_in[:, LQ + LKV:LQ + LKV + ROPE]
    swap = np.r_[ROPE // 2:ROPE, 0:ROPE // 2]
    uq = w["w_uq"][0].reshape(LQ, H, QKD)
    ukv = w["w_ukv"][0].reshape(LKV, H, NOPE + VD)
    cols = lambda v: v.reshape(-1, P).T
    conv0 = LQ + LKV + ROPE
    conv_cols = w_in[:, conv0:conv0 + 3 * CW].reshape(D, 3, CW // P, P).transpose(0, 2, 1, 3).reshape(D, -1)
    slabs = np.concatenate([w_in[:, :LQ + LKV], kr, kr[:, swap], kr, kr[:, swap], conv_cols, w_in[:, conv0 + 3 * CW:]], 1)
    arrays = {
        "x": w["x"][0], "mem": w["mem"][0], "positions": w["positions"],
        "g_mix": w["g_mix"], "g_xattn": w["g_xattn"], "g_mem": w["g_mem"], "g_moe": w["g_moe"], "g_final": w["g_final"].reshape(1, D),
        "w_slabs": slabs.reshape(KD, P, -1, P).transpose(2, 1, 0, 3),
        "w_uq": np.concatenate([uq[:, :, :NOPE].reshape(LQ, -1), uq[:, :, NOPE:].reshape(LQ, -1), uq[:, :, NOPE:][:, :, swap].reshape(LQ, -1)], 1),
        "w_uk": ukv[:, :, :NOPE].reshape(LKV, -1), "w_uv": ukv[:, :, NOPE:].reshape(LKV, -1),
        "w_branch_a": w["w_branch_a"][0], "w_branch_b": w["w_branch_b"][0], "w_out": w["w_out"][0],
        "w_q_mem": w["w_q_mem"][0], "w_kv_mem": w["w_kv_mem"][0], "w_o_mem": w["w_o_mem"][0],
        "w_r": np.concatenate([w["w_router_group"][0], w["w_router_expert"][0]], 1),
        "b_r": np.concatenate([w["b_router_group"], w["b_router_expert"]], 1),
        "w_gate_up": w["w_gate_up"][0], "w_down": w["w_down"][0],
        "vecs": np.concatenate([w["conv_w"][0].T.reshape(CW // P, P, 3).transpose(1, 0, 2).reshape(P, -1),
                                cols(w["b_gate"][0]), cols(w["g_cq"][0]), cols(w["g_ckv"][0])], 1),
        "consts": constants(),
    }
    nc = bacc.Bacc("TRN2", target_bir_lowering=False, num_devices=1)
    feed, aps = {}, {}
    for name, v in arrays.items():
        v = np.ascontiguousarray(v)
        feed[f"in_{name}"] = v
        aps[name] = nc.dram_tensor(f"in_{name}", v.shape, mybir.dt.from_np(v.dtype), kind="ExternalInput").ap()
    out = nc.dram_tensor("out", (T, D), F32, kind="ExternalOutput").ap()
    program(nc, aps, out)
    r = run_bass_kernel_spmd(nc, [feed], core_ids=[0])
    return r.results[0]["out"].reshape(1, T, D)
```
